# Optimizing a Trainium2 kernel written in Bass

```python
import jax
import jax.numpy as jnp
from jax import lax
import numpy as np

D_MODEL = 1024
BATCH = 1
SEQ = 1024
DEPTH = 2
DEC_BATCH = 8
DEC_SEQ = 16
PAST_LEN = 256

CHUNK = 64
QBLOCK = 128
RMS_EPS = 1e-6
NEG_BIG = -1e30

RWKV_HEADS = 8
RWKV_HEAD_DIM = 64
RWKV_WIDTH = RWKV_HEADS * RWKV_HEAD_DIM
DECAY_LORA = 64
AAA_LORA = 64
RWKV_SHIFT_WIDTH = 3 * RWKV_WIDTH + DECAY_LORA + AAA_LORA
GN_EPS = 64e-5

MLA_HEADS = 8
MLA_NOPE = 64
MLA_ROPE = 32
MLA_V = 64
MLA_Q_LORA = 384
MLA_KV_LORA = 256
MLA_WIDTH = MLA_HEADS * MLA_V
ROPE_THETA = 10000.0

SB_HEADS = 8
SB_HEAD_DIM = 64
SB_WIDTH = SB_HEADS * SB_HEAD_DIM

N_BRANCH = 3
IN_SIZES = (RWKV_SHIFT_WIDTH, RWKV_WIDTH, MLA_Q_LORA, MLA_KV_LORA, MLA_ROPE, MLA_WIDTH,
            SB_WIDTH, SB_WIDTH, SB_WIDTH, SB_WIDTH, N_BRANCH * D_MODEL)
D_IN = (RWKV_SHIFT_WIDTH + RWKV_WIDTH + MLA_Q_LORA + MLA_KV_LORA + MLA_ROPE + MLA_WIDTH
        + 4 * SB_WIDTH + N_BRANCH * D_MODEL)
RWKV_SIZES = (RWKV_WIDTH, RWKV_WIDTH, RWKV_WIDTH, DECAY_LORA, AAA_LORA)

kernel_name = "hybrid_rwkv7_mla_stickbreaking_stream_step"

def _split(x, sizes):
    return jnp.split(x, np.cumsum(sizes)[:-1].tolist(), axis=-1)

def rms_norm(x, g, eps=RMS_EPS):
    xf = x.astype(jnp.float32)
    return xf * lax.rsqrt(jnp.mean(xf * xf, axis=-1, keepdims=True) + eps) * g.astype(jnp.float32)

def rope(x, pos):
    half = MLA_ROPE // 2
    inv = ROPE_THETA ** (-jnp.arange(half, dtype=jnp.float32) / half)
    ang = pos.astype(jnp.float32)[..., None] * inv
    cos, sin = jnp.cos(ang), jnp.sin(ang)
    x1, x2 = x[..., :half], x[..., half:]
    return jnp.concatenate([x1 * cos - x2 * sin, x1 * sin + x2 * cos], axis=-1)

def sweep_queries(fn, q, q_pos):
    T = q.shape[1]
    if T <= QBLOCK or T % QBLOCK:
        return fn(q, q_pos)
    nb = T // QBLOCK
    qb = jnp.moveaxis(q.reshape(q.shape[0], nb, QBLOCK, *q.shape[2:]), 1, 0)
    pb = q_pos.reshape(nb, QBLOCK)
    ob = lax.map(lambda args: fn(args[0], args[1]), (qb, pb))
    return jnp.moveaxis(ob, 0, 1).reshape(q.shape[0], T, *ob.shape[3:])

def chunk_softmax_attn(q, k, v, q_pos, k_pos):
    s = jnp.einsum('bqhd,bshd->bhqs', q, k).astype(jnp.float32) * (q.shape[-1] ** -0.5)
    mask = (k_pos // CHUNK)[None, :] <= (q_pos // CHUNK)[:, None]
    p = jax.nn.softmax(jnp.where(mask, s, NEG_BIG), axis=-1)
    return jnp.einsum('bhqs,bshd->bqhd', p, v.astype(jnp.float32))

def stick_breaking_attn(q, k, v, q_pos, k_pos):
    z = jnp.einsum('bqhd,bshd->bhqs', q, k).astype(jnp.float32) * (q.shape[-1] ** -0.5)
    mask = k_pos[None, :] < q_pos[:, None]
    log_1mb = jnp.where(mask, jax.nn.log_sigmoid(-z), 0.0)
    suffix = lax.cumsum(log_1mb, axis=3, reverse=True) - log_1mb
    a = jnp.where(mask, jnp.exp(jax.nn.log_sigmoid(z) + suffix), 0.0)
    return jnp.einsum('bhqs,bshd->bqhd', a, v.astype(jnp.float32))

def rwkv7_branch(p_shift, past_shift, S0, P, l):
    B, T, _ = p_shift.shape
    H, N = RWKV_HEADS, RWKV_HEAD_DIM
    prev = jnp.concatenate([past_shift.astype(p_shift.dtype), p_shift[:, :-1]], axis=1)
    xs = p_shift + (prev - p_shift) * P['rwkv_mu'][l]
    r, k, v, wd, ad = _split(xs, RWKV_SIZES)
    w_log = -jax.nn.softplus(-(P['rwkv_w0'][l] + jnp.tanh(wd) @ P['rwkv_w_up'][l])) - 0.5
    a = jax.nn.sigmoid(P['rwkv_a0'][l] + ad @ P['rwkv_a_up'][l])
    hd = lambda t: t.astype(jnp.float32).reshape(B, T, H, N)
    r, k, v, a = hd(r), hd(k), hd(v), hd(a)
    decay = jnp.exp(-jnp.exp(hd(w_log)))
    kk = k * P['rwkv_k_k'][l].reshape(H, N)
    kk = kk / jnp.maximum(jnp.sqrt(jnp.sum(kk * kk, axis=-1, keepdims=True)), 1e-12)
    k = k * (1.0 + (a - 1.0) * P['rwkv_k_a'][l].reshape(H, N))

    def step(S, inp):
        r_t, w_t, k_t, v_t, kk_t, a_t = inp
        sa = jnp.einsum('bhij,bhj->bhi', S, -kk_t)
        S = (S * w_t[:, :, None, :] + sa[..., :, None] * (kk_t * a_t)[..., None, :]
             + v_t[..., :, None] * k_t[..., None, :])
        return S, jnp.einsum('bhij,bhj->bhi', S, r_t)

    S_fin, ys = lax.scan(step, S0.astype(jnp.float32),
                         tuple(jnp.moveaxis(t, 1, 0) for t in (r, decay, k, v, kk, a)))
    y = jnp.moveaxis(ys, 0, 1)
    mu = jnp.mean(y, axis=-1, keepdims=True)
    var = jnp.mean(jnp.square(y - mu), axis=-1, keepdims=True)
    y = ((y - mu) * lax.rsqrt(var + GN_EPS)).reshape(B, T, RWKV_WIDTH) * P['rwkv_gn_g'][l] + P['rwkv_gn_b'][l]
    bonus = jnp.sum(r * k * P['rwkv_r_k'][l].reshape(H, N), axis=-1, keepdims=True) * v
    return y + bonus.reshape(B, T, RWKV_WIDTH), S_fin, p_shift[:, -1:]

def mla_branch(cq_raw, ckv_raw, kr_raw, past_ckv, past_kr, q_pos, k_pos, P, l):
    B, T, _ = cq_raw.shape
    q = (rms_norm(cq_raw, P['mla_q_norm'][l]) @ P['mla_w_uq'][l]).reshape(B, T, MLA_HEADS, MLA_NOPE + MLA_ROPE)
    q_nope = rms_norm(q[..., :MLA_NOPE], P['mla_qn_nope'][l])
    q_rope = rope(rms_norm(q[..., MLA_NOPE:], P['mla_qn_rope'][l]), q_pos[:, None])
    c_kv = rms_norm(ckv_raw, P['mla_kv_norm'][l])
    k_rope = rope(rms_norm(kr_raw, P['mla_kn_rope'][l]), q_pos)
    ckv_all = jnp.concatenate([past_ckv, c_kv], axis=1)
    kr_all = jnp.concatenate([past_kr, k_rope], axis=1)
    S = ckv_all.shape[1]
    kv = (ckv_all @ P['mla_w_ukv'][l]).reshape(B, S, MLA_HEADS, MLA_NOPE + MLA_V)
    k_nope = rms_norm(kv[..., :MLA_NOPE], P['mla_kn_nope'][l])
    v = kv[..., MLA_NOPE:]
    k = jnp.concatenate([k_nope, jnp.broadcast_to(kr_all[:, :, None, :].astype(jnp.float32),
                                                  (B, S, MLA_HEADS, MLA_ROPE))], axis=-1)
    qf = jnp.concatenate([q_nope, q_rope], axis=-1)
    o = sweep_queries(lambda qb, pb: chunk_softmax_attn(qb, k, v, pb, k_pos), qf, q_pos)
    return o.reshape(B, T, MLA_WIDTH), c_kv, k_rope

def sb_branch(q_raw, k_raw, v_raw, past_k, past_v, q_pos, k_pos):
    B, T, _ = q_raw.shape
    q = q_raw.reshape(B, T, SB_HEADS, SB_HEAD_DIM)
    k_new = k_raw.reshape(B, T, SB_HEADS, SB_HEAD_DIM)
    v_new = v_raw.reshape(B, T, SB_HEADS, SB_HEAD_DIM)
    k_all = jnp.concatenate([past_k, k_new], axis=1)
    v_all = jnp.concatenate([past_v, v_new], axis=1)
    o = sweep_queries(lambda qb, pb: stick_breaking_attn(qb, k_all, v_all, pb, k_pos), q, q_pos)
    return o.reshape(B, T, SB_WIDTH), k_new, v_new

def layer(x, c, q_pos, past, P, l):
    S0, shift0, ckv0, kr0, k0, v0 = past
    past_len = ckv0.shape[1]
    k_pos = jnp.concatenate([jnp.arange(past_len, dtype=jnp.int32), q_pos])
    mod = jax.nn.silu(c.astype(jnp.float32)) @ P['w_ada'][l] + P['b_ada'][l]
    shift, scale, gate = jnp.split(mod[:, None, :], 3, axis=-1)
    h = rms_norm(x, P['norm_g'][l]) * (1.0 + scale) + shift
    proj = h @ P['w_in'][l]
    pr, zA, cq, ckv, kr, zB, sq, sk, sv, zC, gates = _split(proj, IN_SIZES)
    yA, S1, shift1 = rwkv7_branch(pr, shift0, S0, P, l)
    yB, ckv1, kr1 = mla_branch(cq, ckv, kr, ckv0, kr0, q_pos, k_pos, P, l)
    yC, k1, v1 = sb_branch(sq, sk, sv, k0, v0, q_pos, k_pos)
    gA, gB, gC = jnp.split(jax.nn.sigmoid(gates), 3, axis=-1)
    merged = (gA * ((yA * jax.nn.silu(zA)) @ P['w_br_rwkv'][l])
              + gB * ((yB * jax.nn.silu(zB)) @ P['w_br_mla'][l])
              + gC * ((yC * jax.nn.silu(zC)) @ P['w_br_sb'][l]))
    x = x + gate * (merged @ P['w_out'][l])
    return x, (S1, shift1, ckv1, kr1, k1, v1)

def trunk(x, c, q_pos, pasts, P):
    new = []
    for l in range(DEPTH):
        x, st = layer(x, c, q_pos, pasts[l], P, l)
        new.append(st)
    stacked = [jnp.stack([st[i] for st in new], axis=0) for i in range(6)]
    return x, stacked

def setup_inputs(seed: int = 0) -> dict:
    key = jax.random.key(seed)
    ks = iter(jax.random.split(key, 48))
    f32 = jnp.float32

    def nrm(shape, scale=1.0):
        return jax.random.normal(next(ks), shape, f32) * scale

    def gain(shape):
        return 1.0 + nrm(shape, 0.05)

    D, L = D_MODEL, DEPTH
    return {
        'x_prompt': nrm((BATCH, SEQ, D)),
        'x_sample': nrm((DEC_BATCH, DEC_SEQ, D)),
        'state_rwkv_wkv': nrm((L, DEC_BATCH, RWKV_HEADS, RWKV_HEAD_DIM, RWKV_HEAD_DIM), 0.5),
        'state_rwkv_shift': nrm((L, DEC_BATCH, 1, RWKV_SHIFT_WIDTH)),
        'cache_mla_ckv': nrm((L, DEC_BATCH, PAST_LEN, MLA_KV_LORA)),
        'cache_mla_krope': nrm((L, DEC_BATCH, PAST_LEN, MLA_ROPE)),
        'cache_sb_k': nrm((L, DEC_BATCH, PAST_LEN, SB_HEADS, SB_HEAD_DIM)),
        'cache_sb_v': nrm((L, DEC_BATCH, PAST_LEN, SB_HEADS, SB_HEAD_DIM)),
        'c_prompt': nrm((BATCH, D)),
        'c_sample': nrm((DEC_BATCH, D)),
        'w_ada': nrm((L, D, 3 * D), 0.5 * D ** -0.5),
        'b_ada': nrm((L, 3 * D), 0.02),
        'norm_g': gain((L, D)),
        'w_in': nrm((L, D, D_IN), D ** -0.5),
        'rwkv_mu': jax.random.uniform(next(ks), (L, RWKV_SHIFT_WIDTH), f32),
        'rwkv_w0': nrm((L, RWKV_WIDTH), 0.5),
        'rwkv_w_up': nrm((L, DECAY_LORA, RWKV_WIDTH), 0.5 * DECAY_LORA ** -0.5),
        'rwkv_a0': nrm((L, RWKV_WIDTH), 0.5),
        'rwkv_a_up': nrm((L, AAA_LORA, RWKV_WIDTH), 0.5 * AAA_LORA ** -0.5),
        'rwkv_k_k': 0.85 + nrm((L, RWKV_WIDTH), 0.05),
        'rwkv_k_a': gain((L, RWKV_WIDTH)),
        'rwkv_r_k': nrm((L, RWKV_WIDTH), 0.1),
        'rwkv_gn_g': gain((L, RWKV_WIDTH)),
        'rwkv_gn_b': nrm((L, RWKV_WIDTH), 0.02),
        'w_br_rwkv': nrm((L, RWKV_WIDTH, D), RWKV_WIDTH ** -0.5),
        'mla_q_norm': gain((L, MLA_Q_LORA)),
        'mla_w_uq': nrm((L, MLA_Q_LORA, MLA_HEADS * (MLA_NOPE + MLA_ROPE)), MLA_Q_LORA ** -0.5),
        'mla_kv_norm': gain((L, MLA_KV_LORA)),
        'mla_w_ukv': nrm((L, MLA_KV_LORA, MLA_HEADS * (MLA_NOPE + MLA_V)), MLA_KV_LORA ** -0.5),
        'mla_qn_nope': gain((L, MLA_NOPE)),
        'mla_qn_rope': gain((L, MLA_ROPE)),
        'mla_kn_nope': gain((L, MLA_NOPE)),
        'mla_kn_rope': gain((L, MLA_ROPE)),
        'w_br_mla': nrm((L, MLA_WIDTH, D), MLA_WIDTH ** -0.5),
        'w_br_sb': nrm((L, SB_WIDTH, D), SB_WIDTH ** -0.5),
        'w_out': nrm((L, D, D), D ** -0.5),
    }

def reference(x_prompt, x_sample, state_rwkv_wkv, state_rwkv_shift, cache_mla_ckv, cache_mla_krope,
              cache_sb_k, cache_sb_v, c_prompt, c_sample, w_ada, b_ada, norm_g, w_in, rwkv_mu, rwkv_w0,
              rwkv_w_up, rwkv_a0, rwkv_a_up, rwkv_k_k, rwkv_k_a, rwkv_r_k, rwkv_gn_g, rwkv_gn_b, w_br_rwkv,
              mla_q_norm, mla_w_uq, mla_kv_norm, mla_w_ukv, mla_qn_nope, mla_qn_rope, mla_kn_nope,
              mla_kn_rope, w_br_mla, w_br_sb, w_out):
    P = dict(w_ada=w_ada, b_ada=b_ada, norm_g=norm_g, w_in=w_in, rwkv_mu=rwkv_mu, rwkv_w0=rwkv_w0,
             rwkv_w_up=rwkv_w_up, rwkv_a0=rwkv_a0, rwkv_a_up=rwkv_a_up, rwkv_k_k=rwkv_k_k,
             rwkv_k_a=rwkv_k_a, rwkv_r_k=rwkv_r_k, rwkv_gn_g=rwkv_gn_g, rwkv_gn_b=rwkv_gn_b,
             w_br_rwkv=w_br_rwkv, mla_q_norm=mla_q_norm, mla_w_uq=mla_w_uq, mla_kv_norm=mla_kv_norm,
             mla_w_ukv=mla_w_ukv, mla_qn_nope=mla_qn_nope, mla_qn_rope=mla_qn_rope,
             mla_kn_nope=mla_kn_nope, mla_kn_rope=mla_kn_rope, w_br_mla=w_br_mla, w_br_sb=w_br_sb,
             w_out=w_out)
    Bp, Tp = x_prompt.shape[0], x_prompt.shape[1]
    Bs, Ts = x_sample.shape[0], x_sample.shape[1]
    past_len = cache_mla_ckv.shape[2]
    dt = x_prompt.dtype

    empty = (jnp.zeros((Bp, RWKV_HEADS, RWKV_HEAD_DIM, RWKV_HEAD_DIM), jnp.float32),
             jnp.zeros((Bp, 1, RWKV_SHIFT_WIDTH), dt),
             jnp.zeros((Bp, 0, MLA_KV_LORA), dt),
             jnp.zeros((Bp, 0, MLA_ROPE), dt),
             jnp.zeros((Bp, 0, SB_HEADS, SB_HEAD_DIM), dt),
             jnp.zeros((Bp, 0, SB_HEADS, SB_HEAD_DIM), dt))
    pos_p = jnp.arange(Tp, dtype=jnp.int32)
    y_prompt, st_p = trunk(x_prompt, c_prompt, pos_p, [empty] * DEPTH, P)
    wkv_p, shift_p, ckv_p, krope_p, sbk_p, sbv_p = st_p

    pasts_s = [(state_rwkv_wkv[l], state_rwkv_shift[l], cache_mla_ckv[l], cache_mla_krope[l],
                cache_sb_k[l], cache_sb_v[l]) for l in range(DEPTH)]
    pos_s = past_len + jnp.arange(Ts, dtype=jnp.int32)
    y_sample, st_s = trunk(x_sample, c_sample, pos_s, pasts_s, P)
    wkv_s, shift_s, ckv_s, krope_s, sbk_s, sbv_s = st_s

    return (y_prompt, y_sample, wkv_p, shift_p, ckv_p, krope_p, sbk_p, sbv_p,
            wkv_s, shift_s, ckv_s, krope_s, sbk_s, sbv_s)


_drawn_inputs = setup_inputs


def setup_inputs(seed=0):
    import zlib

    import numpy as np

    out = dict(_drawn_inputs(seed))
    spreads = {}
    factors = {'cache_mla_ckv': 3.894,
     'cache_mla_krope': 7.368,
     'cache_sb_k': 4.172,
     'rwkv_k_k': 3.707,
     'rwkv_gn_g': 7.599,
     'rwkv_gn_b': 8.0,
     'mla_q_norm': 8.0,
     'mla_w_uq': 4.059,
     'mla_qn_nope': 8.0,
     'mla_qn_rope': 8.0,
     'mla_kn_nope': 8.0}
    for name, (base, spread) in spreads.items():
        noise = np.random.default_rng([zlib.crc32(name.encode()), seed]).standard_normal(out[name].shape)
        drawn = base * np.exp(spread * noise) if base else spread * noise
        out[name] = jnp.asarray(drawn.astype(out[name].dtype))
    for name, factor in factors.items():
        out[name] = (out[name] * factor).astype(out[name].dtype)
    return out
```

```python
from contextlib import ExitStack, contextmanager

import numpy as np
import concourse.bass as bass
from concourse import mybir

ALU = mybir.AluOpType
ACT = mybir.ActivationFunctionType
AX = mybir.AxisListType
F32 = mybir.dt.float32

P = 128
D = 1024
KD = D // P
L = 2
TP = 1024
NB = 8
TS = 16
PAST = 256
T = TP + NB * TS
NT = T // P
NPT = TP // P
TG = 384
NTG = T // TG
HP = 4
RW = 1664
W0 = 512
QL, KVL, RP = 384, 256, 32
QK = 96
SK = PAST + TS
LAYERS = L
NEG = -1e30
PADW = 1 + TP + NB * (TS + 1)
G_R, G_K, G_V, G_LORA, G_ZA, G_ZB, G_SQ, G_SK, G_ZC, G_GATE = 0, 4, 8, 12, 13, 17, 21, 25, 29, 33
NCH = G_GATE + 3 * KD
ROWS = T + NB * PAST
NRT = ROWS // P
E_HALF = float(np.exp(-0.5))

CONST_WIDTHS = [("ident", P), ("blockones", P), ("block32", P), ("negtri", P), ("negones", P), ("sbkeep", P), ("sbneg", P),
                ("mask_p", 2 * P), ("mask_s", 2 * P), ("masi_p", 2 * P), ("masi_s", 2 * P),
                ("dn_p", 2 * P), ("dn_s", 2 * P), ("dt16", P),
                ("selp", P), ("sels", P), ("seqof", NB), ("negsel", P), ("rot", P),
                ("eps", 4), ("headscale", 2), ("reset", T), ("cosT", T), ("sinT", T), ("cross", NB * TS), ("crossneg", NB * TS)]
CONST_AT, CONST_COLS = {}, 0
for _n, _w in CONST_WIDTHS:
    CONST_AT[_n] = (CONST_COLS, _w)
    CONST_COLS += _w
CONST_RESIDENT = CONST_AT["reset"][0]


def shape_constants():
    i = np.arange(P)
    row, col = i[:, None], i[None, :]
    f = lambda m: np.asarray(m, np.float32)
    c = {}
    c["ident"] = f(row == col)
    c["blockones"] = f(row // 64 == col // 64)
    c["block32"] = f(row // 32 == col // 32)
    c["negtri"] = -f(row >= col)
    c["negones"] = -np.ones((P, P), np.float32)
    c["sbkeep"] = f(row < col)
    c["sbneg"] = NEG * f(row >= col)
    for n, chunk in (("p", 64), ("s", TS)):
        same = row // chunk == col // chunk
        up, upi = f(same & (row < col)), f(same & (row <= col))
        c["mask_" + n] = np.concatenate([up, up], 1)
        c["masi_" + n] = np.concatenate([upi, upi], 1)
        low = same & (row > col)
        d16 = low & (row // 16 == col // 16)
        c["dn_" + n] = np.concatenate([f(d16), f(low & ~d16)], 1)
    c["dt16"] = f((row // 16 == col // 16) & (row < col))
    t = np.arange(T)
    first = np.where(t < TP, t % 64 == 0, (t - TP) % TS == 0)
    c["reset"] = np.broadcast_to(f(~first)[None], (P, T))
    c["selp"] = f(row == 0) * np.ones((1, P), np.float32)
    c["sels"] = f(row - 1 == col // TS)
    c["seqof"] = f(row // TS == np.arange(NB)[None])
    c["negsel"] = NEG * f(row != col // TS)
    c["rot"] = f((col % 32 >= 16) & (row == col - 16)) - f((col % 32 < 16) & (row == col + 16))
    c["headscale"] = 0.125 * f(row // 64 == np.arange(2)[None])
    c["eps"] = np.broadcast_to(np.array([[1e-6, 64e-5, 10 * np.log(2.0), 0]], np.float32), (P, 4))
    pos = np.where(t < TP, t, PAST + (t - TP) % TS).astype(np.float32)
    inv = (np.float32(10000.0) ** (-np.arange(16, dtype=np.float32) / np.float32(16))).astype(np.float32)
    ang = (inv[i % 16][:, None] * pos[None, :]).astype(np.float32)
    c["cosT"], c["sinT"] = np.cos(ang), np.sin(ang)
    q = np.arange(NB * TS)[None, :]
    c["cross"] = f(row < q % TS)
    c["crossneg"] = NEG * (1 - c["cross"])
    return np.concatenate([c[n] for n, _ in CONST_WIDTHS], 1).astype(np.float32)


class InOrder:

    def __init__(self, eng, own):
        self.eng, self.own, self.n = eng, own, {}

    def __call__(self, ins, sem=None):
        sem = self.own if sem is None else sem
        self.n[sem.num] = self.n.get(sem.num, 0) + 1
        ins.then_inc(sem, 1)
        self.eng.wait_ge(sem, self.n[sem.num])


class Stages:

    def __init__(self, nc):
        self.nc, self.k, self.first = nc, 0, None

    @contextmanager
    def stage(self, *names):
        nc = self.nc
        self.k += 1
        sems = []
        for n in names:
            sems.append(nc.alloc_semaphore(f"{n}_{self.k}", **({} if self.first is None else {"num": self.first + len(sems)})))
            self.first = sems[0].num
        lo, hi = sems[0].num, sems[-1].num
        assert hi - lo == len(sems) - 1
        with ExitStack() as ctx:
            def sb(name, shape, dt=F32):
                return ctx.enter_context(nc.sbuf_tensor(f"{name}_{self.k}", shape, dt))
            with nc.Block() as block:
                yield block, sb, sems
        nc.gpsimd.sem_clear(range(lo, hi + 1))
        nc.all_engine_barrier()
        for s in sems:
            nc.release_semaphore(s)


def build(nc, A, O, only=None):
    with ExitStack() as ctx:
        def sbt(name, shape, dt=F32):
            return ctx.enter_context(nc.sbuf_tensor(name, shape, dt))

        S = Stages(nc)
        ps = ctx.enter_context(nc.psum_tensor("banks", [P, 8, 512], F32))
        X = sbt("x_resident", [P, NT, D])
        hT = sbt("hT", [P, KD, T])
        cst = sbt("constants", [P, CONST_RESIDENT])
        gates = sbt("gate_rows", [P, 2, D])

        def con(name):
            a, w = CONST_AT[name]
            if a >= CONST_RESIDENT:
                return A["consts"][:, a:a + w]
            return cst[:, a:a + w]

        yg = nc.dram_tensor("y_gated", (3, HP, P, T), F32).ap()

        with S.stage("consts_loaded", "x_loaded") as (block, sb, (consts_loaded, x_loaded)):
            @block.sync
            def _(sp):
                sp.dma_start(cst[:, :], A["consts"][:, 0:CONST_RESIDENT]).then_inc(consts_loaded, 16)
                sp.dma_start(X[:, 0:NPT, :], A["x_prompt"][0].rearrange("(n p) d -> p n d", p=P)).then_inc(x_loaded, 16)
                sp.dma_start(X[:, NPT, :], A["x_sample"].rearrange("b t d -> (b t) d")).then_inc(x_loaded, 16)
                sp.wait_ge(consts_loaded, 16)
                sp.wait_ge(x_loaded, 32)

        with nc.Fori(0, LAYERS) as l:
            modulation(nc, S, A, l, ps, con, gates, X, hT)
            rwkv(nc, S, A, O, l, ps, con, hT, yg)
            latent_attention(nc, S, A, O, l, ps, con, hT, yg)
            stick_breaking(nc, S, A, O, l, ps, con, hT, yg)
            merge(nc, S, A, l, ps, con, hT, yg, gates, X)

        with S.stage("y_stored") as (block, sb, (y_stored,)):
            @block.sync
            def _(sp):
                sp.dma_start(O["y_prompt"][0].rearrange("(n p) d -> p n d", p=P), X[:, 0:NPT, :]).then_inc(y_stored, 16)
                sp.dma_start(O["y_sample"].rearrange("b t d -> (b t) d"), X[:, NPT, :]).then_inc(y_stored, 16)
                sp.wait_ge(y_stored, 32)


def modulation(nc, S, A, l, ps, con, gates, X, hT):
    ident = con("ident")
    NC = 1 + NB
    with ExitStack() as ctx:
        mod = ctx.enter_context(nc.sbuf_tensor("mod", [NC, 3 * D], F32))
        shiftT = ctx.enter_context(nc.sbuf_tensor("shiftT", [P, KD, NC], F32))
        scaleT = ctx.enter_context(nc.sbuf_tensor("scaleT", [P, KD, NC], F32))
        names = ("c_loaded", "w0_loaded", "w1_loaded", "tanh_done", "silu_done", "cT_ready", "cT_copied",
                 "mod_ready", "mod_added", "modT_ready", "modT_copied", "rows_ready", "rows_copied", "vec")
        with S.stage(*names) as (block, sb, (c_loaded, w0_loaded, w1_loaded, tanh_done, silu_done, cT_ready, cT_copied,
                                             mod_ready, mod_added, modT_ready, modT_copied, rows_ready, rows_copied, vec)):
            c = sb("c", [NC, D])
            th = sb("c_tanh", [NC, D])
            cT = sb("cT", [P, KD, NC])
            bada = sb("b_ada", [NC, 3 * D])
            g = sb("norm_g", [P, KD])
            w = [sb("w_ada0", [P, KD, 512]), sb("w_ada1", [P, KD, 512])]
            w_loaded = [w0_loaded, w1_loaded]
            NG = 3 * D // 512

            @block.sync
            def _(sp):
                sp.dma_start(c[:, :], A["c_all"]).then_inc(c_loaded, 16)
                sp.dma_start(bada[:, :], A["b_ada"][l].broadcast_to([NC, 3 * D])).then_inc(c_loaded, 16)
                sp.dma_start(g[:, :], A["norm_g"][l]).then_inc(c_loaded, 16)
                for j in range(NG):
                    if j >= 2:
                        sp.wait_ge(mod_ready, j - 1)
                    sp.dma_start(w[j % 2][:, :, :], A["w_ada"][l, j]).then_inc(w_loaded[j % 2], 16)

            @block.scalar
            def _(act):
                act.wait_ge(c_loaded, 48)
                nc.scalar.activation(th[:, :], c[:, :], ACT.Tanh, scale=0.5).then_inc(tanh_done, 1)

            @block.vector
            def _(dve):
                own = InOrder(dve, vec)
                dve.wait_ge(tanh_done, 1)
                own(nc.vector.tensor_scalar(th[:, :], th[:, :], 1.0, 0.5, ALU.add, ALU.mult))
                nc.vector.tensor_tensor(c[:, :], c[:, :], th[:, :], ALU.mult).then_inc(silu_done, 1)
                dve.wait_ge(cT_ready, 1)
                nc.vector.tensor_copy(cT[:, :, :], ps[:, 0, 0:KD * NC].rearrange("p (k c) -> p k c", c=NC)).then_inc(cT_copied, 1)
                for j in range(NG):
                    dve.wait_ge(mod_ready, j + 1)
                    nc.vector.tensor_tensor(mod[:, 512 * j:512 * j + 512], ps[0:NC, 1 + j % 2, :],
                                            bada[:, 512 * j:512 * j + 512], ALU.add).then_inc(mod_added, 1)
                dve.wait_ge(modT_ready, 1)
                nc.vector.tensor_copy(shiftT[:, :, :], ps[:, 0, 0:KD * NC].rearrange("p (k c) -> p k c", c=NC)).then_inc(modT_copied, 1)
                nc.vector.scalar_tensor_tensor(scaleT[:, :, :], ps[:, 0, KD * NC:2 * KD * NC].rearrange("p (k c) -> p k c", c=NC),
                                               1.0, g[:, :].unsqueeze(2).broadcast_to([P, KD, NC]), ALU.add, ALU.mult).then_inc(modT_copied, 1)
                for j in range(4):
                    dve.wait_ge(rows_ready, j + 1)
                    nc.vector.tensor_copy(gates[:, j // 2, 512 * (j % 2):512 * (j % 2) + 512], ps[:, 3 + j, :]).then_inc(rows_copied, 1)

            @block.tensor
            def _(pe):
                pe.wait_ge(silu_done, 1)
                for k in range(KD):
                    last = nc.tensor.transpose(ps[:, 0, k * NC:(k + 1) * NC], c[:, P * k:P * k + P], ident[0:NC, 0:NC])
                last.then_inc(cT_ready, 1)
                pe.wait_ge(cT_copied, 1)
                for j in range(NG):
                    pe.wait_ge(w_loaded[j % 2], 16 * (j // 2 + 1))
                    if j >= 2:
                        pe.wait_ge(mod_added, j - 1)
                    for k in range(KD):
                        last = nc.tensor.matmul(ps[0:NC, 1 + j % 2, :], cT[:, k, :], w[j % 2][:, k, :], start=(k == 0), stop=(k == KD - 1))
                    last.then_inc(mod_ready, 1)
                pe.wait_ge(mod_added, NG)
                for k in range(2 * KD):
                    last = nc.tensor.transpose(ps[:, 0, k * NC:(k + 1) * NC], mod[:, P * k:P * k + P], ident[0:NC, 0:NC])
                last.then_inc(modT_ready, 1)
                for j in range(4):
                    sel = con("selp") if j < 2 else con("sels")
                    nc.tensor.matmul(ps[:, 3 + j, :], sel[0:NC, :], mod[:, 2 * D + 512 * (j % 2):2 * D + 512 * (j % 2) + 512],
                                     start=True, stop=True).then_inc(rows_ready, 1)

        names = ("squares_summed", "rstd_done", "xn_done", "h_transposed", "h_written", "act_own", "vec")
        with S.stage(*names) as (block, sb, (squares_summed, rstd_done, xn_done, h_transposed, h_written, act_own, vec)):
            junk = sb("squares", [P, D])
            ss = sb("sum_squares", [P, NT])
            xn = [sb("xn0", [P, D]), sb("xn1", [P, D])]
            tmp = sb("h_sample", [P, KD, P])

            @block.scalar
            def _(act):
                own = InOrder(act, act_own)
                for i in range(NT):
                    own(nc.scalar.activation(junk[:, :], X[:, i, :], ACT.Square, accum_out=ss[:, i:i + 1]))
                own(nc.scalar.activation(ss[:, :], ss[:, :], ACT.Sqrt, scale=1.0 / D, bias=con("eps")[:, 0:1]))
                nc.scalar.activation(junk[:, 0:1], ss[:, 0:1], ACT.Copy).then_inc(squares_summed, 1)
                act.wait_ge(rstd_done, 1)
                for i in range(NT):
                    if i >= 2:
                        act.wait_ge(h_transposed, i - 1)
                    nc.scalar.activation(xn[i % 2][:, :], X[:, i, :], ACT.Copy, scale=ss[:, i:i + 1]).then_inc(xn_done, 1)

            @block.tensor
            def _(pe):
                for i in range(NT):
                    pe.wait_ge(xn_done, i + 1)
                    if i >= 2:
                        pe.wait_ge(h_written, i - 1)
                    for k in range(KD):
                        last = nc.tensor.transpose(ps[:, 4 * (i % 2) + k // 4, P * (k % 4):P * (k % 4) + P], xn[i % 2][:, P * k:P * k + P], ident)
                    last.then_inc(h_transposed, 1)

            @block.vector
            def _(dve):
                own = InOrder(dve, vec)
                dve.wait_ge(squares_summed, 1)
                nc.vector.reciprocal(ss[:, :], ss[:, :]).then_inc(rstd_done, 1)
                for i in range(NT):
                    dve.wait_ge(h_transposed, i + 1)
                    if i < NPT:
                        for k in range(KD):
                            last = nc.vector.tensor_scalar(hT[:, k, P * i:P * i + P], ps[:, 4 * (i % 2) + k // 4, P * (k % 4):P * (k % 4) + P],
                                                           scaleT[:, k, 0:1], shiftT[:, k, 0:1], ALU.mult, ALU.add)
                        last.then_inc(h_written, 1)
                    else:
                        for k in range(KD):
                            src = ps[:, 4 * (i % 2) + k // 4, P * (k % 4):P * (k % 4) + P].rearrange("p (b t) -> p b t", t=TS)
                            own(nc.vector.tensor_tensor(tmp[:, k, :].rearrange("p (b t) -> p b t", t=TS), src,
                                                        scaleT[:, k, 1:NC].unsqueeze(2).broadcast_to([P, NB, TS]), ALU.mult))
                            own(nc.vector.tensor_tensor(hT[:, k, P * i:P * i + P].rearrange("p (b t) -> p b t", t=TS),
                                                        tmp[:, k, :].rearrange("p (b t) -> p b t", t=TS),
                                                        shiftT[:, k, 1:NC].unsqueeze(2).broadcast_to([P, NB, TS]), ALU.add))


def project(nc, pe, ps, banks, w, hT, ready, free, first, waits=None):
    for g in range(NTG):
        n = first + g
        if n >= len(banks):
            pe.wait_ge(free, n - len(banks) + 1)
        for k in range(KD):
            last = nc.tensor.matmul(ps[:, banks[n % len(banks)], 0:TG], w[:, k, :], hT[:, k, TG * g:TG * g + TG],
                                    start=(k == 0), stop=(k == KD - 1))
        last.then_inc(ready, 1)


def pad_parts(g):
    a = TG * g
    if a + TG <= TP:
        return [(slice(0, TG), None, slice(1 + a, 1 + a + TG))]
    return [(slice(0, TP - a), None, slice(1 + a, 1 + TP)), (slice(TP - a, TG), "s", slice(1 + TP, PADW))]


def seqs(ap):
    return ap.rearrange("p (b t) -> p b t", t=TS + 1)


def rwkv(nc, S, A, O, l, ps, con, hT, yg):
    ident = con("ident")
    with ExitStack() as ctx:
        lora = ctx.enter_context(nc.sbuf_tensor("lora", [P, T], F32))

        names = ("loaded", "projected", "evacuated", "shifted", "stored", "vec")
        with S.stage(*names) as (block, sb, (loaded, projected, evacuated, shifted, stored, vec)):
            w = sb("w_lora_in", [P, KD, P])
            pad = sb("lora_padded", [P, PADW])
            d = sb("lora_difference", [P, T])
            mu = sb("lora_mu", [P, 1])

            @block.sync
            def _(sp):
                sp.dma_start(w[:, :, :], A["w_cols"][l, G_LORA]).then_inc(loaded, 16)
                sp.dma_start(mu[:, :], A["mu_lora"][l]).then_inc(loaded, 16)
                sp.dma_start(seqs(pad[:, 1 + TP:PADW])[:, :, 0], A["shift0"][l, 12], allow_slow_non_contiguous=True).then_inc(loaded, 16)
                sp.wait_ge(evacuated, NTG + 1)
                sp.dma_start(O["shift_p"][l, 12], pad[:, TP:TP + 1]).then_inc(stored, 16)
                sp.dma_start(O["shift_s"][l, 12], seqs(pad[:, 1 + TP:PADW])[:, :, TS], allow_slow_non_contiguous=True).then_inc(stored, 16)
                sp.wait_ge(stored, 32)

            @block.tensor
            def _(pe):
                pe.wait_ge(loaded, 48)
                project(nc, pe, ps, (0, 1, 2), w, hT, projected, evacuated, 0)

            @block.scalar
            def _(act):
                for g in range(NTG):
                    act.wait_ge(projected, g + 1)
                    for a, s, b in pad_parts(g):
                        src = ps[:, g, a]
                        if s is None:
                            ins = nc.scalar.activation(pad[:, b], src, ACT.Copy)
                        else:
                            ins = nc.scalar.activation(seqs(pad[:, b])[:, :, 1:], src.rearrange("p (b t) -> p b t", t=TS), ACT.Copy)
                        ins.then_inc(evacuated, 1)
                act.wait_ge(shifted, 1)
                nc.scalar.activation(lora[0:64, :], lora[0:64, :], ACT.Tanh)

            @block.vector
            def _(dve):
                own = InOrder(dve, vec)
                own(nc.vector.memset(pad[:, 0:1], 0.0))
                dve.wait_ge(loaded, 48)
                dve.wait_ge(evacuated, NTG + 1)
                token_shift(nc, own, pad, d, mu[:, 0:1], lora)
                nc.vector.engine_nop().then_inc(shifted, 1)

        with nc.Fori(0, HP) as h:
            rwkv_pair(nc, S, A, O, l, h, ps, con, hT, yg, lora)


def token_shift(nc, own, pad, d, mu, out):
    cur = [pad[:, 1:1 + TP], seqs(pad[:, 1 + TP:PADW])[:, :, 1:]]
    prev = [pad[:, 0:TP], seqs(pad[:, 1 + TP:PADW])[:, :, 0:TS]]
    dd = [d[:, 0:TP], d[:, TP:T].rearrange("p (b t) -> p b t", t=TS)]
    oo = [out[:, 0:TP], out[:, TP:T].rearrange("p (b t) -> p b t", t=TS)]
    for i in range(2):
        own(nc.vector.tensor_tensor(dd[i], prev[i], cur[i], ALU.subtract))
    for i in range(2):
        own(nc.vector.scalar_tensor_tensor(oo[i], dd[i], mu, cur[i], ALU.mult, ALU.add))


def rwkv_pair(nc, S, A, O, l, h, ps, con, hT, yg, lora):
    ident = con("ident")
    V = nc.vector
    with ExitStack() as ctx:
        def keep(name, shape):
            return ctx.enter_context(nc.sbuf_tensor(name, shape, F32))

        AR = keep("a_and_r", [P, 2, T])
        BK = keep("b_and_k", [P, 2, T])
        Bt, Kt = BK[:, 0, :], BK[:, 1, :]
        vT = keep("v_transposed", [P, T])
        bonus = keep("bonus", [P, T])
        zs = keep("silu_z", [P, T])
        pend = keep("decay_of_chunk", [P, TP // 64 + NB])
        par = keep("parameters", [P, 12])
        MU, W0C, A0, KK, KA, RK, GG, GB = 0, 3, 4, 5, 6, 7, 8, 9

        names = ("loaded", "projected", "evacuated", "stored", "lora_out", "lora_read", "act_in", "act_out",
                 "pe_in", "pe_out", "act_own", "vec")
        with S.stage(*names) as (block, sb, (loaded, projected, evacuated, stored, lora_out, lora_read, act_in, act_out,
                                             pe_in, pe_out, act_own, vec)):
            w = [sb(f"w_piece{j}", [P, KD, P]) for j in range(2)]
            pads = [sb(f"padded{j}", [P, PADW]) for j in range(3)]
            t = [sb(f"temp{j}", [P, T]) for j in range(2)]
            rT = sb("r_shifted", [P, T])
            kT = sb("k_shifted", [P, T])
            aT = sb("a_gate", [P, T])
            reset = sb("chunk_reset", [P, T])
            wl = sb("w_lora", [P, P])
            zT = AR[:, 0, :]
            base = (G_R, G_K, G_V, G_ZA)
            NEV = NTG + 1

            @block.sync
            def _(sp):
                sp.dma_start(reset[:, :], con("reset")).then_inc(loaded, 16)
                sp.dma_start(par[:, 0:10], A["rw_par"][l, h]).then_inc(loaded, 16)
                sp.dma_start(wl[:, :], A["w_lora"][l, h]).then_inc(loaded, 16)
                for j in range(3):
                    sp.dma_start(seqs(pads[j][:, 1 + TP:PADW])[:, :, 0], A["shift0"][l, 4 * j + h],
                                 allow_slow_non_contiguous=True).then_inc(loaded, 16)
                for j in range(2):
                    sp.dma_start(w[j][:, :, :], A["w_cols"][l, base[j] + h]).then_inc(loaded, 16)
                for j in range(2, 4):
                    sp.wait_ge(projected, NTG * (j - 1))
                    sp.wait_ge(loaded, 16 * (6 + j))
                    sp.dma_start(w[j % 2][:, :, :], A["w_cols"][l, base[j] + h]).then_inc(loaded, 16)
                sp.wait_ge(evacuated, 3 * NEV)
                for j in range(3):
                    sp.dma_start(O["shift_p"][l, 4 * j + h], pads[j][:, TP:TP + 1]).then_inc(stored, 16)
                    sp.dma_start(O["shift_s"][l, 4 * j + h], seqs(pads[j][:, 1 + TP:PADW])[:, :, TS],
                                 allow_slow_non_contiguous=True).then_inc(stored, 16)
                sp.wait_ge(stored, 96)

            @block.tensor
            def _(pe):
                for j in range(4):
                    pe.wait_ge(loaded, 16 * 8 if j < 2 else 16 * (7 + j))
                    for g in range(NTG):
                        n = NTG * j + g
                        if n >= 6:
                            m = n - 6
                            pe.wait_ge(evacuated, NEV * (m // NTG) + (m % NTG) + 1 + (m % NTG == NTG - 1))
                        for k in range(KD):
                            last = nc.tensor.matmul(ps[:, n % 6, 0:TG], w[j % 2][:, k, :], hT[:, k, TG * g:TG * g + TG],
                                                    start=(k == 0), stop=(k == KD - 1))
                        last.then_inc(projected, 1)
                for q in range(2):
                    for g in range(NTG):
                        n = NTG * q + g
                        if n >= 2:
                            pe.wait_ge(lora_read, n - 1)
                        nc.tensor.matmul(ps[:, 6 + n % 2, 0:TG], wl[64 * q:64 * q + 64, :],
                                         lora[64 * q:64 * q + 64, TG * g:TG * g + TG], start=True, stop=True).then_inc(lora_out, 1)
                for q in range(2):
                    pe.wait_ge(pe_in, q + 1)
                    if q == 0:
                        pe.wait_ge(evacuated, 3 * NEV + NTG)
                    for g in range(NTG):
                        last = nc.tensor.matmul(ps[:, 3 * q + g, 0:TG], con("blockones"), t[0][:, TG * g:TG * g + TG], start=True, stop=True)
                    last.then_inc(pe_out, 1)

            @block.scalar
            def _(act):
                own = InOrder(act, act_own)
                for n in range(3 * NTG):
                    j, g = divmod(n, NTG)
                    act.wait_ge(projected, n + 1)
                    for a, s, b in pad_parts(g):
                        src = ps[:, n % 6, a]
                        if s is None:
                            ins = nc.scalar.activation(pads[j][:, b], src, ACT.Copy)
                        else:
                            ins = nc.scalar.activation(seqs(pads[j][:, b])[:, :, 1:], src.rearrange("p (b t) -> p b t", t=TS), ACT.Copy)
                        ins.then_inc(evacuated, 1)
                for g in range(NTG):
                    act.wait_ge(projected, 3 * NTG + g + 1)
                    nc.scalar.activation(zT[:, TG * g:TG * g + TG], ps[:, (3 * NTG + g) % 6, 0:TG], ACT.Copy).then_inc(evacuated, 1)
                act.wait_ge(evacuated, 3 * NEV + NTG)
                nc.scalar.activation(zs[:, :], zT, ACT.Tanh, scale=0.5).then_inc(act_out, 1)
                act.wait_ge(act_in, 1)
                for q, dst in ((0, t[0]), (1, aT)):
                    for g in range(NTG):
                        act.wait_ge(lora_out, NTG * q + g + 1)
                        nc.scalar.activation(dst[:, TG * g:TG * g + TG], ps[:, 6 + (NTG * q + g) % 2, 0:TG], ACT.Tanh,
                                             scale=0.5, bias=par[:, 10 + q:11 + q]).then_inc(lora_read, 1)
                act.wait_ge(act_in, 2)
                own(nc.scalar.activation(AR[:, 0, :], t[0][:, :], ACT.Exp))
                own(nc.scalar.activation(AR[:, 1, :], t[1][:, :], ACT.Exp))
                own(nc.scalar.activation(Bt, t[1][:, :], ACT.Exp, scale=-1.0))
                nc.scalar.activation(Kt[:, 0:1], Bt[:, 0:1], ACT.Copy).then_inc(act_out, 1)
                act.wait_ge(pe_out, 1)
                act.wait_ge(act_in, 3)
                for g in range(NTG):
                    own(nc.scalar.activation(t[1][:, TG * g:TG * g + TG], ps[:, g, 0:TG], ACT.Sqrt))
                nc.scalar.activation(Kt[:, 0:1], t[1][:, 0:1], ACT.Copy).then_inc(act_out, 1)

            @block.vector
            def _(dve):
                own = InOrder(dve, vec)
                for j in range(3):
                    own(V.memset(pads[j][:, 0:1], 0.0))
                dve.wait_ge(loaded, 16 * 8)
                own(V.tensor_scalar(par[:, 10:12], par[:, W0C:W0C + 2], 0.5, None, ALU.mult), act_in)
                dve.wait_ge(evacuated, 3 * NEV)
                for j, dst in enumerate((rT, kT, vT)):
                    token_shift(nc, own, pads[j], t[1], par[:, MU + j:MU + j + 1], dst)
                dve.wait_ge(act_out, 1)
                own(V.tensor_scalar(zs[:, :], zs[:, :], 1.0, 0.5, ALU.add, ALU.mult))
                own(V.tensor_tensor(zs[:, :], zs[:, :], zT, ALU.mult))
                dve.wait_ge(lora_read, 2 * NTG)
                own(V.tensor_scalar(t[0][:, :], t[0][:, :], 1.0, -0.5 * E_HALF, ALU.add, ALU.mult))
                own(V.tensor_scalar(aT[:, :], aT[:, :], 1.0, 0.5, ALU.add, ALU.mult))
                own(V.tensor_tensor_scan(t[1][:, :], reset[:, :], t[0][:, :], 0.0, ALU.mult, ALU.add))
                own(V.tensor_tensor(t[0][:, :], t[1][:, :], t[0][:, :], ALU.subtract), act_in)
                dve.wait_ge(act_out, 2)
                own(V.tensor_copy(pend[:, 0:TP // 64], AR[:, 1, 63:TP:64]))
                own(V.tensor_copy(pend[:, TP // 64:], AR[:, 1, TP + TS - 1:T:TS]), act_in)
                kk = pads[0][:, 0:T]
                dve.wait_ge(stored, 96)
                own(V.tensor_scalar(kk, kT[:, :], par[:, KK:KK + 1], None, ALU.mult))
                own(V.tensor_tensor(t[0][:, :], kk, kk, ALU.mult), pe_in)
                nk = pads[1][:, 0:T]
                own(V.scalar_tensor_tensor(nk, aT[:, :], -1.0, kT[:, :], ALU.add, ALU.mult))
                own(V.scalar_tensor_tensor(nk, nk, par[:, KA:KA + 1], kT[:, :], ALU.mult, ALU.add))
                dve.wait_ge(act_out, 3)
                own(V.tensor_scalar(t[1][:, :], t[1][:, :], 1e-12, None, ALU.max))
                own(V.reciprocal(t[1][:, :], t[1][:, :]))
                own(V.tensor_tensor(kk, kk, t[1][:, :], ALU.mult))
                own(V.scalar_tensor_tensor(t[0][:, :], rT[:, :], par[:, RK:RK + 1], nk, ALU.mult, ALU.mult), pe_in)
                own(V.scalar_tensor_tensor(AR[:, 0, :], kk, -1.0, AR[:, 0, :], ALU.mult, ALU.mult))
                own(V.tensor_tensor(Kt, nk, Bt, ALU.mult))
                own(V.tensor_tensor(Bt, kk, Bt, ALU.mult))
                own(V.tensor_tensor(Bt, aT[:, :], Bt, ALU.mult))
                own(V.tensor_tensor(AR[:, 1, :], rT[:, :], AR[:, 1, :], ALU.mult))
                dve.wait_ge(pe_out, 2)
                for g in range(NTG):
                    own(V.tensor_tensor(bonus[:, TG * g:TG * g + TG], ps[:, 3 + g, 0:TG], vT[:, TG * g:TG * g + TG], ALU.mult))

        TM = keep("b_k_v_rows", [P, NT, 4, P])
        SI = keep("scores_r", [P, NT, 2, 2 * P])
        WT = keep("w_solved", [P, NT, P])
        Z = keep("z_solved", [P, NT, P])
        Y = Z

        names = ("rows_ready", "rows_copied", "head_split", "scores_ready", "masked", "diag_ready", "power_ready", "power_copied",
                 "akv_ready", "akv_copied", "step_ready", "step_added", "xt_ready", "xt_copied", "w_rows", "w_ready", "w_copied", "act_own", "vec")
        with S.stage(*names) as (block, sb, (rows_ready, rows_copied, head_split, scores_ready, masked, diag_ready, power_ready, power_copied,
                                             akv_ready, akv_copied, step_ready, step_added, xt_ready, xt_copied, w_rows, w_ready, w_copied, act_own, vec)):
            BKz = [sb(f"bk_of_head{s}", [P, 2, 2, P]) for s in range(2)]
            SC = [sb(f"scores_a{s}", [P, 2, 2 * P]) for s in range(2)]
            PW = [[sb(f"power{s}{i}", [P, 2, 2 * P]) for i in range(3)] for s in range(2)]
            P8 = [sb(f"power8_{s}", [P, 2, P]) for s in range(2)]
            R = [sb(f"rhs{s}", [P, 2, 2 * P]) for s in range(2)]
            XT = [sb(f"xT{s}", [P, 2, P]) for s in range(2)]
            Q = [sb(f"q{s}", [P, 2, P]) for s in range(2)]
            WP = [sb(f"w_rows{s}", [P, P]) for s in range(2)]
            srcs = (AR[:, 0, :], Bt, Kt, vT)
            pairs = [[i, i + 1] if i + 1 < NT else [i] for i in range(0, NT, 2)]

            def two(ap):
                return ap.rearrange("p (h n) -> p h n", h=2)

            def power(pe, i, n):
                s, b = i % 2, 4 * (i % 2)
                for hh in range(2):
                    m, mt = PW[s][n][:, hh, 0:P], PW[s][n][:, hh, P:2 * P]
                    if n < 2:
                        nc.tensor.matmul(ps[:, b + 3, 2 * P * hh:2 * P * hh + P], mt, m, start=True, stop=True)
                        last = nc.tensor.matmul(ps[:, b + 3, 2 * P * hh + P:2 * P * hh + 2 * P], m, mt, start=True, stop=True)
                    else:
                        last = nc.tensor.matmul(ps[:, b + 3, P * hh:P * hh + P], m, mt, start=True, stop=True)
                last.then_inc(power_ready, 1)

            def power_count(grp, i, n):
                return 3 * grp[0] + len(grp) * (n - 1) + grp.index(i) + 1

            def step_count(grp, i, n):
                p = [x for x in grp if x != NPT]
                if n <= 4:
                    return 7 * grp[0] + len(grp) * (n - 1) + grp.index(i) + 1
                return 7 * grp[0] + len(grp) * 4 + len(p) * (n - 5) + grp.index(i) + 1

            @block.tensor
            def _(pe):
                for grp in pairs:
                    if grp[0] >= 2:
                        pe.wait_ge(w_copied, grp[0])
                    for i in grp:
                        b = 4 * (i % 2)
                        for q in range(4):
                            last = nc.tensor.transpose(ps[:, b + 3, P * q:P * q + P], srcs[q][:, P * i:P * i + P], ident)
                        last.then_inc(rows_ready, 1)
                        c = slice(P * i, P * i + P)
                        z = BKz[i % 2]
                        pe.wait_ge(head_split, i + 1)
                        for hh in range(2):
                            for q in range(2):
                                out = ps[:, b + hh, :].rearrange("p (e q n) -> p e q n", e=2, q=2)[:, :, q, :]
                                nc.tensor.matmul(out, z[:, hh, q, :], AR[:, :, c], start=True, stop=True)
                        last = nc.tensor.matmul(ps[:, b + 2, 0:2 * P], AR[:, 0, c], z[:, :, 0, :], start=True, stop=True)
                        last.then_inc(scores_ready, 1)
                    for i in grp:
                        s, b = i % 2, 4 * (i % 2)
                        pe.wait_ge(masked, i + 1)
                        for hh in range(2):
                            last = nc.tensor.matmul(ps[:, b + 2, 2 * P + 64 * hh:2 * P + 64 * hh + 64], SC[s][:, hh, P:2 * P],
                                                    TM[:, i, 3, 64 * hh:64 * hh + 64], start=True, stop=True)
                        last.then_inc(akv_ready, 1)
                        pe.wait_ge(rows_copied, i + 1)
                        power(pe, i, 0)
                    for st in range(4):
                        for i in grp:
                            s, b = i % 2, 4 * (i % 2)
                            if st == 0:
                                pe.wait_ge(akv_copied, i + 1)
                            else:
                                pe.wait_ge(step_added, step_count(grp, i, st))
                                pe.wait_ge(power_copied, power_count(grp, i, st))
                            for hh in range(2):
                                lt = PW[s][st][:, hh, P:2 * P] if st < 3 else P8[s][:, hh, :]
                                last = nc.tensor.matmul(two(ps[:, b + st % 2, :])[:, hh, :], lt, R[s][:, hh, :], start=True, stop=True)
                            last.then_inc(step_ready, 1)
                            if st < 2:
                                pe.wait_ge(power_copied, power_count(grp, i, st + 1))
                                power(pe, i, st + 1)
                    for i in grp:
                        if i == NPT:
                            continue
                        s, b = i % 2, 4 * (i % 2)
                        pe.wait_ge(step_added, step_count(grp, i, 4))
                        for hh in range(2):
                            last = nc.tensor.transpose(ps[:, b + 2, P * hh:P * hh + P], R[s][:, hh, P:2 * P], ident)
                        last.then_inc(xt_ready, 1)
                    for st in range(3):
                        for i in grp:
                            if i == NPT:
                                continue
                            s, b = i % 2, 4 * (i % 2)
                            if st == 0:
                                pe.wait_ge(xt_copied, i + 1)
                            else:
                                pe.wait_ge(step_added, step_count(grp, i, 4 + st))
                            for hh in range(2):
                                rhs = R[s][:, hh, 0:P] if st == 0 else Q[s][:, hh, :]
                                last = nc.tensor.matmul(ps[:, b + st % 2, P * hh:P * hh + P], XT[s][:, hh, :], rhs, start=True, stop=True)
                            last.then_inc(step_ready, 1)
                    for i in grp:
                        s, b = i % 2, 4 * (i % 2)
                        pe.wait_ge(w_rows, i + 1)
                        nc.tensor.transpose(ps[:, b + 2, 3 * P:4 * P], WP[s][:, :], ident).then_inc(w_ready, 1)

            @block.scalar
            def _(act):
                for grp in pairs:
                    for i in grp:
                        s, b = i % 2, 4 * (i % 2)
                        if i >= 2:
                            act.wait_ge(masked, i - 1)
                        for hh in range(2):
                            ins = nc.scalar.activation(BKz[s][:, hh, :, :], BK[:, :, P * i:P * i + P], ACT.Copy,
                                                       scale=con("blockones")[:, 64 * hh:64 * hh + 1])
                        ins.then_inc(head_split, 1)
                        act.wait_ge(rows_ready, i + 1)
                        nc.scalar.activation(TM[:, i, :, :].rearrange("p q n -> p (q n)"), ps[:, b + 3, :], ACT.Copy).then_inc(rows_copied, 1)
                    for n in range(3):
                        for i in grp:
                            s, b = i % 2, 4 * (i % 2)
                            act.wait_ge(power_ready, power_count(grp, i, n + 1))
                            if n < 2:
                                nc.scalar.activation(PW[s][n + 1][:, :, :], two(ps[:, b + 3, :]), ACT.Copy).then_inc(power_copied, 1)
                            else:
                                nc.scalar.activation(P8[s][:, :, :], ps[:, b + 3, 0:2 * P].rearrange("p (h n) -> p h n", h=2), ACT.Copy).then_inc(power_copied, 1)
                    for i in grp:
                        if i == NPT:
                            continue
                        s, b = i % 2, 4 * (i % 2)
                        act.wait_ge(xt_ready, i + 1)
                        nc.scalar.activation(XT[s][:, :, :], ps[:, b + 2, 0:2 * P].rearrange("p (h n) -> p h n", h=2), ACT.Copy).then_inc(xt_copied, 1)
                    for i in grp:
                        s, b = i % 2, 4 * (i % 2)
                        act.wait_ge(w_ready, i + 1)
                        nc.scalar.activation(WT[:, i, :], ps[:, b + 2, 3 * P:4 * P], ACT.Copy).then_inc(w_copied, 1)

            @block.vector
            def _(dve):
                own = InOrder(dve, vec)

                def bc(m):
                    return m.unsqueeze(1).broadcast_to([P, 2, m.shape[1]])

                for grp in pairs:
                    for i in grp:
                        s, b = i % 2, 4 * (i % 2)
                        k = "s" if i == NPT else "p"
                        dve.wait_ge(scores_ready, i + 1)
                        both = ps[:, b:b + 2, :]
                        own(V.tensor_tensor(SC[s][:, :, :], both[:, :, 0:2 * P], bc(con("mask_" + k)), ALU.mult))
                        own(V.tensor_tensor(SI[:, i, :, :], both[:, :, 2 * P:4 * P], bc(con("masi_" + k)), ALU.mult))
                        low = ps[:, b + 2, 0:2 * P].rearrange("p (h n) -> p h n", h=2)
                        dn = con("dn_" + k)
                        own(V.tensor_tensor(PW[s][0][:, :, 0:P], low, bc(dn[:, 0:P]), ALU.mult))
                        own(V.tensor_tensor(R[s][:, :, P:2 * P], low, bc(dn[:, P:2 * P]), ALU.mult))
                        dve.wait_ge(rows_copied, i + 1)
                        own(V.tensor_copy(R[s][:, :, 0:64], TM[:, i, 0, :].rearrange("p (h n) -> p h n", h=2)))
                        own(V.tensor_tensor(PW[s][0][:, :, P:2 * P], SC[s][:, :, 0:P], bc(con("dt16")), ALU.mult), masked)
                    for i in grp:
                        s, b = i % 2, 4 * (i % 2)
                        dve.wait_ge(akv_ready, i + 1)
                        own(V.tensor_copy(R[s][:, :, 64:P], ps[:, b + 2, 2 * P:3 * P].rearrange("p (h n) -> p h n", h=2)), akv_copied)
                    for st in range(4):
                        for i in grp:
                            s, b = i % 2, 4 * (i % 2)
                            dve.wait_ge(step_ready, step_count(grp, i, st + 1))
                            own(V.tensor_tensor(R[s][:, :, :], R[s][:, :, :], two(ps[:, b + st % 2, :]), ALU.add), step_added)
                    for st in range(3):
                        for i in grp:
                            if i == NPT:
                                continue
                            s, b = i % 2, 4 * (i % 2)
                            dve.wait_ge(step_ready, step_count(grp, i, st + 5))
                            own(V.tensor_tensor(Q[s][:, :, :], R[s][:, :, 0:P], ps[:, b + st % 2, 0:2 * P].rearrange("p (h n) -> p h n", h=2), ALU.add), step_added)
                    for i in grp:
                        s, b = i % 2, 4 * (i % 2)
                        src = R[s][:, :, 0:P] if i == NPT else Q[s][:, :, :]
                        own(V.tensor_copy(Z[:, i, :].rearrange("p (h n) -> p h n", h=2), src[:, :, 64:P]))
                        own(V.tensor_copy(WP[s][:, :].rearrange("p (h n) -> p h n", h=2), src[:, :, 0:64]), w_rows)

        names = ("state_loaded", "state_out", "u_ready", "u_added", "y_ready", "y_copied", "s_ready", "s_scaled", "vec", "act_own")
        with S.stage(*names) as (block, sb, (state_loaded, state_out, u_ready, u_added, y_ready, y_copied, s_ready, s_scaled, vec, act_own)):
            ST = sb("state", [P, P])
            S0 = sb("sample_states", [P, NB * 64])
            SN = sb("sample_states_new", [P, NB * 64])
            U = sb("u_rows", [P, 2, P])
            wide = [sb(f"by_sequence{i}", [P, NB, 64]) for i in range(4)]
            y0 = sb("y_from_state", [P, P])
            NCK = TP // 64

            @block.sync
            def _(sp):
                sp.dma_start(S0[:, :], A["state0"][l, h]).then_inc(state_loaded, 16)
                sp.wait_ge(s_scaled, NCK + 1)
                for hh in range(2):
                    hc = slice(64 * hh, 64 * hh + 64)
                    sp.dma_start(O["wkv_p"][l, h, hc], ST[hc, hc]).then_inc(state_out, 16)
                sp.wait_ge(s_scaled, NCK + 2)
                sp.dma_start(O["wkv_s"][l, h], SN[:, :]).then_inc(state_out, 16)
                sp.wait_ge(state_out, 48)

            @block.tensor
            def _(pe):
                mm = nc.tensor.matmul
                for i in range(NPT):
                    ybank = 2 + i % 2
                    if i >= 2:
                        pe.wait_ge(y_copied, i - 1)
                    for hh in range(2):
                        hc = slice(64 * hh, 64 * hh + 64)
                        mm(ps[:, ybank, hc], SI[:, i, hh, P:2 * P], TM[:, i, 3, hc], start=(hh == 0), stop=False, skip_group_check=True)
                    for c in range(2):
                        n = 2 * i + c
                        tc = slice(64 * c, 64 * c + 64)
                        tok = slice(P * i + 64 * c, P * i + 64 * c + 64)
                        pe.wait_ge(s_scaled, n + 1)
                        mm(ps[tc, 4 + n % 2, 0:P], WT[:, i, tc], ST[:, :], start=True, stop=True).then_inc(u_ready, 1)
                        mm(ps[tc, ybank, 0:P], AR[:, 1, tok], ST[:, :], start=False, stop=False, skip_group_check=True)
                        mm(ps[:, 6 + n % 2, 0:P], ident, ST[:, :], start=True, stop=False)
                        mm(ps[:, 6 + n % 2, 0:P], TM[tc, i, 2, :], TM[tc, i, 3, :], start=False, stop=False)
                        pe.wait_ge(u_added, n + 1)
                        mm(ps[:, 6 + n % 2, 0:P], TM[tc, i, 1, :], U[tc, i % 2, :], start=False, stop=True).then_inc(s_ready, 1)
                    for hh in range(2):
                        hc = slice(64 * hh, 64 * hh + 64)
                        last = mm(ps[:, ybank, hc], SI[:, i, hh, 0:P], U[:, i % 2, hc], start=False, stop=True, skip_group_check=True)
                    last.then_inc(y_ready, 1)
                i = NPT
                pe.wait_ge(state_loaded, 16)
                for hh in range(2):
                    hc = slice(64 * hh, 64 * hh + 64)
                    mm(ps[:, hh, :], WT[hc, i, :], S0[hc, :], start=True, stop=True)
                    last = mm(ps[:, 4 + hh, :], AR[hc, 1, P * i:P * i + P], S0[hc, :], start=True, stop=True)
                last.then_inc(u_ready, 1)
                pe.wait_ge(u_added, 2 * NPT + 1)
                pe.wait_ge(y_copied, NPT)
                for hh in range(2):
                    hc = slice(64 * hh, 64 * hh + 64)
                    mm(ps[:, 2, hc], SI[:, i, hh, P:2 * P], TM[:, i, 3, hc], start=(hh == 0), stop=False, skip_group_check=True)
                for hh in range(2):
                    hc = slice(64 * hh, 64 * hh + 64)
                    last = mm(ps[:, 2, hc], SI[:, i, hh, 0:P], U[:, 0, hc], start=False, stop=True, skip_group_check=True)
                last.then_inc(y_ready, 1)
                for hh in range(2):
                    hc = slice(64 * hh, 64 * hh + 64)
                    pe.wait_ge(u_added, 2 * NPT + 2)
                    mm(ps[hc, 6, :], TM[:, i, 1, hc], wide[hh][:, :, :].rearrange("p b n -> p (b n)"), start=True, stop=False, skip_group_check=True)
                    mm(ps[hc, 6, :], TM[:, i, 2, hc], wide[2 + hh][:, :, :].rearrange("p b n -> p (b n)"), start=False, stop=False, skip_group_check=True)
                    last = mm(ps[hc, 6, :], ident[hc, hc], S0[hc, :], start=False, stop=True, skip_group_check=True)
                last.then_inc(s_ready, 1)

            @block.scalar
            def _(act):
                for i in range(NPT):
                    act.wait_ge(y_ready, i + 1)
                    nc.scalar.activation(Y[:, i, :], ps[:, 2 + i % 2, 0:P], ACT.Copy).then_inc(y_copied, 1)

            @block.vector
            def _(dve):
                own = InOrder(dve, vec)
                own(V.memset(ST[:, :], 0.0), s_scaled)
                for n in range(2 * NPT):
                    i, c = divmod(n, 2)
                    tc = slice(64 * c, 64 * c + 64)
                    dve.wait_ge(u_ready, n + 1)
                    if c == 0 and i >= 2:
                        dve.wait_ge(y_ready, i - 1)
                    own(V.tensor_tensor(U[tc, i % 2, :], Z[tc, i, :], ps[tc, 4 + n % 2, 0:P], ALU.add), u_added)
                    dve.wait_ge(s_ready, n + 1)
                    own(V.scalar_tensor_tensor(ST[:, :], ps[:, 6 + n % 2, 0:P], pend[:, n:n + 1], con("blockones"), ALU.mult, ALU.mult), s_scaled)
                i = NPT
                seq = con("seqof").unsqueeze(2).broadcast_to([P, NB, 64])
                dve.wait_ge(u_ready, 2 * NPT + 1)
                dve.wait_ge(y_ready, NPT)
                for hh in range(2):
                    hc = slice(64 * hh, 64 * hh + 64)
                    for bank, dst in ((hh, U[:, 0, hc]), (4 + hh, y0[:, hc])):
                        own(V.tensor_tensor(wide[0][:, :, :], ps[:, bank, :].rearrange("p (b n) -> p b n", n=64), seq, ALU.mult))
                        own(V.tensor_reduce(dst, wide[0][:, :, :].rearrange("p b n -> p n b"), AX.X, ALU.add))
                own(V.tensor_tensor(U[:, 0, :], U[:, 0, :], Z[:, i, :], ALU.add), u_added)
                for hh in range(2):
                    hc = slice(64 * hh, 64 * hh + 64)
                    own(V.tensor_tensor(wide[hh][:, :, :], U[:, 0, hc].unsqueeze(1).broadcast_to([P, NB, 64]), seq, ALU.mult))
                    own(V.tensor_tensor(wide[2 + hh][:, :, :], TM[:, i, 3, hc].unsqueeze(1).broadcast_to([P, NB, 64]), seq, ALU.mult),
                        u_added if hh == 1 else None)
                dve.wait_ge(y_ready, NPT + 1)
                own(V.tensor_tensor(Y[:, i, :], ps[:, 2, 0:P], y0[:, :], ALU.add))
                dve.wait_ge(s_ready, 2 * NPT + 1)
                own(V.tensor_tensor(SN[:, :].rearrange("p (b n) -> p b n", n=64), ps[:, 6, :].rearrange("p (b n) -> p b n", n=64),
                                    pend[:, NCK:].unsqueeze(2).broadcast_to([P, NB, 64]), ALU.mult), s_scaled)

        names = ("rstd_in", "rstd_out", "y_normed", "y_turned", "y_gated", "y_stored", "vec")
        with S.stage(*names) as (block, sb, (rstd_in, rstd_out, y_normed, y_turned, y_gated, y_stored, vec)):
            sq = sb("centred_squares", [P, NT, 2, 64])
            st = sb("statistics", [P, NT * 2])
            out = sb("y_out", [P, T])
            Yv = Y[:, :, :].rearrange("p i (h n) -> p (i h) n", n=64)
            sqv = sq[:, :, :, :].rearrange("p i h n -> p (i h) n")

            @block.vector
            def _(dve):
                own = InOrder(dve, vec)
                wide = st[:, :].unsqueeze(2).broadcast_to([P, NT * 2, 64])
                own(V.tensor_reduce(st[:, :], Yv, AX.X, ALU.add))
                own(V.tensor_scalar(st[:, :], st[:, :], 1.0 / 64, None, ALU.mult))
                own(V.tensor_tensor(Yv, Yv, wide, ALU.subtract))
                own(V.tensor_tensor(sqv, Yv, Yv, ALU.mult))
                own(V.tensor_reduce(st[:, :], sqv, AX.X, ALU.add), rstd_in)
                dve.wait_ge(rstd_out, 1)
                own(V.reciprocal(st[:, :], st[:, :]))
                own(V.tensor_tensor(Yv, Yv, wide, ALU.mult), y_normed)
                for g in range(NTG):
                    c = slice(TG * g, TG * g + TG)
                    dve.wait_ge(y_turned, g + 1)
                    own(V.tensor_scalar(out[:, c], ps[:, g, 0:TG], par[:, GG:GG + 1], par[:, GB:GB + 1], ALU.mult, ALU.add))
                own(V.tensor_tensor(out[:, :], out[:, :], bonus[:, :], ALU.add))
                own(V.tensor_tensor(out[:, :], out[:, :], zs[:, :], ALU.mult), y_gated)

            @block.scalar
            def _(act):
                act.wait_ge(rstd_in, 1)
                nc.scalar.activation(st[:, :], st[:, :], ACT.Sqrt, scale=1.0 / 64, bias=con("eps")[:, 1:2]).then_inc(rstd_out, 1)

            @block.tensor
            def _(pe):
                pe.wait_ge(y_normed, 1)
                for i in range(NT):
                    last = nc.tensor.transpose(ps[:, i // 3, P * (i % 3):P * (i % 3) + P], Y[:, i, :], ident)
                    if i % 3 == 2:
                        last.then_inc(y_turned, 1)

            @block.sync
            def _(sp):
                sp.wait_ge(y_gated, 1)
                sp.dma_start(yg[0, h], out[:, :]).then_inc(y_stored, 16)
                sp.wait_ge(y_stored, 16)


def gate_and_store(nc, S, A, l, h, ps, con, hT, yg, branch, piece, rows=None, cols=None):
    V = nc.vector
    names = ("w_loaded", "z_ready", "y_turned", "tanh_done", "gated", "stored")
    with S.stage(*names) as (block, sb, (w_loaded, z_ready, y_turned, tanh_done, gated, stored)):
        w = sb("w_z", [P, KD, P])
        th = sb("z_tanh", [P, T])
        out = sb("gated", [P, T])

        @block.sync
        def _(sp):
            sp.dma_start(w[:, :, :], A["w_cols"][l, piece + h]).then_inc(w_loaded, 16)
            sp.wait_ge(gated, 3 * NTG)
            sp.dma_start(yg[branch, h], out[:, :]).then_inc(stored, 16)
            sp.wait_ge(stored, 16)

        @block.tensor
        def _(pe):
            if rows is not None:
                for i in range(NT):
                    last = nc.tensor.transpose(ps[:, 3 + i // 3, P * (i % 3):P * (i % 3) + P], rows[:, i, :], con("ident"))
                last.then_inc(y_turned, 1)
            pe.wait_ge(w_loaded, 16)
            project(nc, pe, ps, (0, 1, 2), w, hT, z_ready, gated, 0)

        @block.scalar
        def _(act):
            for g in range(NTG):
                act.wait_ge(z_ready, g + 1)
                nc.scalar.activation(th[:, TG * g:TG * g + TG], ps[:, g, 0:TG], ACT.Tanh, scale=0.5).then_inc(tanh_done, 1)

        @block.vector
        def _(dve):
            own = InOrder(dve, gated)
            if rows is not None:
                dve.wait_ge(y_turned, 1)
            for g in range(NTG):
                c = slice(TG * g, TG * g + TG)
                y = ps[:, 3 + g, 0:TG] if rows is not None else cols[:, c]
                dve.wait_ge(tanh_done, g + 1)
                own(V.scalar_tensor_tensor(out[:, c], th[:, c], 1.0, ps[:, g, 0:TG], ALU.add, ALU.mult))
                own(V.tensor_scalar(out[:, c], out[:, c], 0.5, None, ALU.mult))
                own(V.tensor_tensor(out[:, c], out[:, c], y, ALU.mult))


GK = 400


def latent_attention(nc, S, A, O, l, ps, con, hT, yg):
    ident = con("ident")
    V = nc.vector
    NL = QL + KVL + RP
    with ExitStack() as ctx:
        latT = ctx.enter_context(nc.sbuf_tensor("latentT", [P, 2, ROWS], F32))
        cqT = ctx.enter_context(nc.sbuf_tensor("cqT", [P, 3, T], F32))

        names = ("loaded", "cached_loaded", "projected", "copied", "squared", "rooted", "normed", "turned", "turned_read", "stored0", "stored1", "kr_stored",
                 "kr_turned", "kr_done", "vec", "act_own")
        with S.stage(*names) as (block, sb, (loaded, cached_loaded, projected, copied, squared, rooted, normed, turned, turned_read, stored0, stored1, kr_stored,
                                             kr_turned, kr_done, vec, act_own)):
            w = sb("w_latent", [P, KD, NL])
            g = sb("latent_gains", [P, NL])
            raw = [sb(f"latent_raw{i}", [P, NL]) for i in range(2)]
            lat = [sb(f"latent{i}", [P, NL]) for i in range(2)]
            junk = sb("latent_squares", [P, QL])
            ss = sb("latent_sums", [P, 2, 3])
            kr = sb("krT", [RP, T])
            kr2 = sb("krT_rotated", [RP, T])
            cs = sb("cos_sin", [RP, 2, T])
            parts = ((0, QL), (QL, QL + KVL), (QL + KVL, NL))

            @block.sync
            def _(sp):
                sp.dma_start(w[:, :, :], A["w_lat"][l]).then_inc(loaded, 16)
                sp.dma_start(g[:, :], A["lat_rows"][l].broadcast_to([P, NL])).then_inc(loaded, 16)
                sp.dma_start(cs[:, 0, :], con("cosT")[0:RP, :]).then_inc(loaded, 16)
                sp.dma_start(cs[:, 1, :], con("sinT")[0:RP, :]).then_inc(loaded, 16)
                sp.dma_start(latT[:, :, T:ROWS], A["ckvT"][l]).then_inc(cached_loaded, 16)
                for i in range(NT):
                    sp.wait_ge(normed, i + 1)
                    sp.dma_start(O["ckv"][l, P * i:P * i + P, :], lat[i % 2][:, QL:QL + KVL]).then_inc((stored0, stored1)[i % 2], 16)
                sp.wait_ge(kr_done, 1)
                sp.dma_start(O["kropeT"][l], kr[:, :]).then_inc(kr_stored, 16)
                sp.wait_ge(stored0, 16 * ((NT + 1) // 2))
                sp.wait_ge(stored1, 16 * (NT // 2))
                sp.wait_ge(kr_stored, 16)
                sp.wait_ge(cached_loaded, 16)

            @block.tensor
            def _(pe):
                pe.wait_ge(loaded, 64)

                def turn(i):
                    pe.wait_ge(normed, i + 1)
                    if i >= 1:
                        pe.wait_ge(turned_read, i)
                    for q in range(3):
                        nc.tensor.transpose(ps[:, 4, P * q:P * q + P], lat[i % 2][:, P * q:P * q + P], ident)
                    for q in range(2):
                        nc.tensor.transpose(ps[:, 5, P * q:P * q + P], lat[i % 2][:, QL + P * q:QL + P * q + P], ident)
                    nc.tensor.transpose(ps[0:RP, 5, 2 * P:3 * P], lat[i % 2][:, QL + KVL:NL], ident).then_inc(turned, 1)

                for i in range(NT):
                    if i >= 2:
                        pe.wait_ge(copied, i - 1)
                    for b, (a, e) in enumerate(((0, QL), (QL, NL))):
                        for k in range(KD):
                            last = nc.tensor.matmul(ps[:, 2 * (i % 2) + b, 0:e - a], hT[:, k, P * i:P * i + P], w[:, k, a:e], start=(k == 0), stop=(k == KD - 1))
                    last.then_inc(projected, 1)
                    if i >= 1:
                        turn(i - 1)
                turn(NT - 1)
                pe.wait_ge(turned_read, NT)
                for q in range(NTG):
                    last = nc.tensor.matmul(ps[0:RP, q, 0:TG], con("rot")[0:RP, 0:RP], kr[:, TG * q:TG * q + TG], start=True, stop=True)
                last.then_inc(kr_turned, 1)

            @block.scalar
            def _(act):
                own = InOrder(act, act_own)

                def norms(i):
                    act.wait_ge(projected, i + 1)
                    if i >= 2:
                        act.wait_ge(normed, i - 1)
                    b = 2 * (i % 2)
                    own(nc.scalar.activation(raw[i % 2][:, 0:QL], ps[:, b, 0:QL], ACT.Copy))
                    own(nc.scalar.activation(raw[i % 2][:, QL:NL], ps[:, b + 1, 0:NL - QL], ACT.Copy), copied)
                    for j, (a, e) in enumerate(parts):
                        own(nc.scalar.activation(junk[:, 0:e - a], raw[i % 2][:, a:e], ACT.Square, scale=float((e - a) ** -0.5), accum_out=ss[:, i % 2, j:j + 1]))
                    nc.scalar.activation(ss[:, i % 2, :], ss[:, i % 2, :], ACT.Sqrt, bias=con("eps")[:, 0:1]).then_inc(rooted, 1)

                norms(0)
                for i in range(NT):
                    if i + 1 < NT:
                        norms(i + 1)
                    c = slice(P * i, P * i + P)
                    act.wait_ge(turned, i + 1)
                    nc.scalar.activation(cqT[:, :, c], ps[:, 4, 0:3 * P].rearrange("p (q n) -> p q n", q=3), ACT.Copy)
                    nc.scalar.activation(latT[:, :, c], ps[:, 5, 0:2 * P].rearrange("p (q n) -> p q n", q=2), ACT.Copy)
                    own(nc.scalar.activation(kr[:, c], ps[0:RP, 5, 2 * P:3 * P], ACT.Copy), turned_read)

            @block.vector
            def _(dve):
                own = InOrder(dve, vec)
                dve.wait_ge(loaded, 64)
                for i in range(NT):
                    dve.wait_ge(rooted, i + 1)
                    own(V.reciprocal(ss[:, i % 2, :], ss[:, i % 2, :]))
                    if i >= 2:
                        dve.wait_ge(turned, i - 1)
                        dve.wait_ge((stored0, stored1)[i % 2], 16 * (i // 2))
                    for j, (a, e) in enumerate(parts):
                        own(V.scalar_tensor_tensor(lat[i % 2][:, a:e], raw[i % 2][:, a:e], ss[:, i % 2, j:j + 1], g[:, a:e], ALU.mult, ALU.mult),
                            normed if j == 2 else None)
                dve.wait_ge(kr_turned, 1)
                for q in range(NTG):
                    c = slice(TG * q, TG * q + TG)
                    own(V.tensor_tensor(kr2[:, c], ps[0:RP, q, 0:TG], cs[:, 1, c], ALU.mult))
                own(V.tensor_tensor(kr[:, :], kr[:, :], cs[:, 0, :], ALU.mult))
                own(V.tensor_tensor(kr[:, :], kr[:, :], kr2[:, :], ALU.add), kr_done)

        with nc.Fori(0, HP) as h:
            latent_pair(nc, S, A, O, l, h, ps, con, hT, latT, cqT, yg)


def latent_pair(nc, S, A, O, l, h, ps, con, hT, latT, cqT, yg):
    ident = con("ident")
    V = nc.vector
    scale = float(QK) ** -0.5
    NS = 2176 // P
    with ExitStack() as ctx:
        def keep(name, shape):
            return ctx.enter_context(nc.sbuf_tensor(name, shape, F32))

        OR = keep("o_rows", [P, NT, P])
        with ExitStack() as inner:
            def hold(name, shape):
                return inner.enter_context(nc.sbuf_tensor(name, shape, F32))

            K = [hold(f"keysT{hh}", [QK, ROWS]) for hh in range(2)]
            Q = [hold(f"queriesT{hh}", [QK, T]) for hh in range(2)]
            VR = hold("values", [P, NRT, P])

            names = ("loaded", "rope_loaded", "raw_ready", "squared", "summed", "logged", "rstd_done", "normed", "v_ready", "v_copied",
                     "rot_ready", "vec", "act_own")
            with S.stage(*names) as (block, sb, (loaded, rope_loaded, raw_ready, squared, summed, logged, rstd_done, normed, v_ready, v_copied,
                                                 rot_ready, vec, act_own)):
                wkv = sb("w_ukv", [P, 2, 2 * P])
                wq = sb("w_uq", [P, 3, 192])
                par = sb("gains", [P, 4])
                sq = [sb(f"squares{i}", [P, GK]) for i in range(2)]
                rs = [sb(f"rstd{i}", [P, GK]) for i in range(2)]
                qr = sb("q_rope", [64, TG])
                qr2 = sb("q_rope_turned", [64, TG])
                cs = sb("cos_sin", [64, 2, T])
                units = [("k", GK * j) for j in range(ROWS // GK)]
                for j in range(NTG):
                    units += [("q", TG * j), ("r", TG * j)]
                nv = (NRT + 3) // 4

                @block.sync
                def _(sp):
                    sp.dma_start(wkv[:, :, :], A["w_ukv"][l, h]).then_inc(loaded, 16)
                    sp.dma_start(wq[:, :, :], A["w_uq"][l, h]).then_inc(loaded, 16)
                    sp.dma_start(par[:, :], A["lat_par"][l]).then_inc(loaded, 16)
                    sp.dma_start(cs[:, 0, :], con("cosT")[0:64, :]).then_inc(loaded, 16)
                    sp.dma_start(cs[:, 1, :], con("sinT")[0:64, :]).then_inc(loaded, 16)
                    for hh in range(2):
                        sp.dma_start(K[hh][64:QK, 0:T], O["kropeT"][l]).then_inc(rope_loaded, 16)
                        sp.dma_start(K[hh][64:QK, T:ROWS], A["krT"][l]).then_inc(rope_loaded, 16)
                    sp.wait_ge(rope_loaded, 64)

                def shape(u):
                    kind, c = units[u]
                    return kind, c, (GK if kind == "k" else TG), (64 if kind == "r" else P)

                @block.tensor
                def _(pe):
                    pe.wait_ge(loaded, 80)

                    def raw(u):
                        kind, c, n, m = shape(u)
                        if u >= 2:
                            pe.wait_ge(normed, u - 1)
                        if kind == "k":
                            for k in range(2):
                                last = nc.tensor.matmul(ps[:, u % 2, 0:n], wkv[:, k, 0:P], latT[:, k, c:c + n], start=(k == 0), stop=(k == 1))
                        else:
                            for k in range(3):
                                last = nc.tensor.matmul(ps[0:m, u % 2, 0:n], wq[:, k, 0:P] if kind == "q" else wq[:, k, P:192], cqT[:, k, c:c + n],
                                                        start=(k == 0), stop=(k == 2))
                        last.then_inc(raw_ready, 1)

                    raw(0)
                    for u in range(len(units)):
                        kind, c, n, m = shape(u)
                        if u + 1 < len(units) and kind != "r":
                            raw(u + 1)
                        if u < nv:
                            if u >= 2:
                                pe.wait_ge(v_copied, u - 1)
                            for i in range(4 * u, min(4 * u + 4, NRT)):
                                for k in range(2):
                                    last = nc.tensor.matmul(ps[:, 4 + u % 2, P * (i % 4):P * (i % 4) + P], latT[:, k, P * i:P * i + P], wkv[:, k, P:2 * P],
                                                            start=(k == 0), stop=(k == 1))
                            last.then_inc(v_ready, 1)
                        pe.wait_ge(squared, u + 1)
                        ones = con("block32")[0:64, 0:64] if kind == "r" else con("blockones")
                        if u >= 2:
                            pe.wait_ge(logged, u - 1)
                        nc.tensor.matmul(ps[0:m, 2 + u % 2, 0:n], ones, sq[u % 2][0:m, 0:n], start=True, stop=True).then_inc(summed, 1)
                        if kind == "r":
                            j = c // TG
                            pe.wait_ge(vec, 1 + 5 * j)
                            nc.tensor.matmul(ps[0:64, 6, 0:TG], con("rot")[0:64, 0:64], qr[:, :], start=True, stop=True).then_inc(rot_ready, 1)
                            if u + 1 < len(units):
                                raw(u + 1)

                @block.scalar
                def _(act):
                    own = InOrder(act, act_own)
                    nc.scalar.preload_act_table_set("natural_log_exp_and_others")
                    for u in range(len(units)):
                        kind, c, n, m = shape(u)
                        act.wait_ge(raw_ready, u + 1)
                        if u >= 2:
                            act.wait_ge(summed, u - 1)
                        nc.scalar.activation(sq[u % 2][0:m, 0:n], ps[0:m, u % 2, 0:n], ACT.Square,
                                             scale=(RP if kind == "r" else 64) ** -0.5).then_inc(squared, 1)
                        if u < nv:
                            act.wait_ge(v_ready, u + 1)
                            e = min(4, NRT - 4 * u)
                            nc.scalar.activation(VR[:, 4 * u:4 * u + e, :].rearrange("p i n -> p (i n)"), ps[:, 4 + u % 2, 0:P * e], ACT.Copy).then_inc(v_copied, 1)
                        act.wait_ge(summed, u + 1)
                        if u >= 2:
                            act.wait_ge(normed, u - 1)
                        own(nc.scalar.activation(rs[u % 2][0:m, 0:n], ps[0:m, 2 + u % 2, 0:n], ACT.Ln, bias=con("eps")[0:m, 0:1]), logged)
                        nc.scalar.activation(rs[u % 2][0:m, 0:n], rs[u % 2][0:m, 0:n], ACT.Exp, scale=-0.5).then_inc(rstd_done, 1)

                @block.vector
                def _(dve):
                    own = InOrder(dve, vec)
                    dve.wait_ge(loaded, 80)
                    for u in range(len(units)):
                        kind, c, n, m = shape(u)
                        dve.wait_ge(rstd_done, u + 1)
                        if kind == "r":
                            own(V.scalar_tensor_tensor(qr[:, :], ps[0:64, u % 2, 0:n], par[0:64, 1:2], rs[u % 2][0:64, 0:n], ALU.mult, ALU.mult))
                            dve.wait_ge(rot_ready, c // TG + 1)
                            own(V.tensor_tensor(qr2[:, :], ps[0:64, 6, 0:TG], cs[:, 1, c:c + n], ALU.mult))
                            own(V.tensor_tensor(qr[:, :], qr[:, :], cs[:, 0, c:c + n], ALU.mult))
                            for hh in range(2):
                                own(V.tensor_tensor(Q[hh][64:QK, c:c + n], qr[32 * hh:32 * hh + 32, :], qr2[32 * hh:32 * hh + 32, :], ALU.add))
                            V.engine_nop().then_inc(normed, 1)
                        else:
                            dst = K if kind == "k" else Q
                            gain = 2 if kind == "k" else 0
                            for hh in range(2):
                                hc = slice(64 * hh, 64 * hh + 64)
                                ins = V.scalar_tensor_tensor(dst[hh][0:64, c:c + n], ps[hc, u % 2, 0:n], par[hc, gain:gain + 1], rs[u % 2][hc, 0:n], ALU.mult, ALU.mult)
                            ins.then_inc(normed, 1)

            names = ("scores_ready", "max_done", "exps_done", "turned", "turned_copied_a", "turned_copied_v", "o_ready", "o_done", "vec", "act_own")
            with S.stage(*names) as (block, sb, (scores_ready, max_done, exps_done, turned, turned_copied_a, turned_copied_v, o_ready, o_done, vec, act_own)):
                E = sb("exponentials", [P, 2, NS * 64])
                ET = [sb(f"exponentialsT{i}", [P, 8, P]) for i in range(2)]
                mx = sb("maximum", [P, 2 * NT])
                nm = sb("minus_maximum", [P, 2 * NT])
                rsum = sb("row_sums", [P, 2 * NT])
                units = [(hh, i) for i in range(NPT) for hh in range(2)]
                NU = len(units)
                flat = E[:, :, :].rearrange("p a n -> p (a n)")
                NGS = (NS + 3) // 4

                def bank2(u):
                    return ps[:, 2 * (u % 2):2 * (u % 2) + 2, :].rearrange("p b n -> p (b n)")

                sample = ps[:, 0:5, :].rearrange("p b n -> p (b n)")

                @block.tensor
                def _(pe):
                    def scores(u):
                        hh, i = units[u]
                        n = P * (i + 1)
                        if u >= 2:
                            pe.wait_ge(exps_done, u - 1)
                        for a in range(0, n, 512):
                            e = min(a + 512, n)
                            last = nc.tensor.matmul(ps[:, 2 * (u % 2) + a // 512, 0:e - a], Q[hh][:, P * i:P * i + P], K[hh][:, a:e], start=True, stop=True)
                        last.then_inc(scores_ready, 1)

                    scores(0)
                    for u in range(NU):
                        hh, i = units[u]
                        if u + 1 < NU:
                            scores(u + 1)
                        pe.wait_ge(exps_done, u + 1)
                        if u >= 1:
                            pe.wait_ge(turned_copied_a, u)
                            pe.wait_ge(turned_copied_v, u)
                        for j in range(i + 1):
                            last = nc.tensor.transpose(ps[:, 4 + j // 4, P * (j % 4):P * (j % 4) + P], E[:, u % 2, P * j:P * j + P], ident)
                        last.then_inc(turned, 1)
                        pe.wait_ge(turned_copied_a, u + 1)
                        pe.wait_ge(turned_copied_v, u + 1)
                        if u >= 2:
                            pe.wait_ge(o_done, u - 1)
                        for j in range(i + 1):
                            last = nc.tensor.matmul(ps[:, 6 + u % 2, 0:64], ET[u % 2][:, j, :], VR[:, j, 64 * hh:64 * hh + 64], start=(j == 0), stop=(j == i))
                        last.then_inc(o_ready, 1)
                    for hh in range(2):
                        if hh == 0:
                            pe.wait_ge(exps_done, NU)
                            pe.wait_ge(turned_copied_a, NU)
                        else:
                            pe.wait_ge(turned_copied_a, NU + NGS)
                            pe.wait_ge(exps_done, NU + 1)
                        for b in range(5):
                            a = TP + NB * TS + 512 * b
                            n = 512 if b < 4 else P
                            if b == 4:
                                a = TP
                            nc.tensor.matmul(ps[:, b, 0:n], Q[hh][:, TP:T], K[hh][:, a:a + n], start=True, stop=False)
                            own_seq = ident[0:NB, 2 * b:2 * b + 2] if b < 4 else ident[0:NB, 0:NB]
                            s = own_seq.shape[1]
                            last = nc.tensor.matmul(ps[:, b, 0:n], con("negsel")[0:NB, :], own_seq.unsqueeze(2).broadcast_to([NB, s, n // s]),
                                                    start=False, stop=True)
                        last.then_inc(scores_ready, 1)
                        pe.wait_ge(exps_done, NU + hh + 1)
                        for j in range(NS):
                            q = j // 4
                            if j % 4 == 0 and q >= 1:
                                pe.wait_ge(turned_copied_a, NU + NGS * hh + q)
                            last = nc.tensor.transpose(ps[:, 5, P * (j % 4):P * (j % 4) + P], flat[:, P * j:P * j + P], ident)
                            if j % 4 == 3 or j == NS - 1:
                                last.then_inc(turned, 1)
                                pe.wait_ge(turned_copied_a, NU + NGS * hh + q + 1)
                                if j < 4:
                                    pe.wait_ge(o_done, NU - 1 + hh)
                                for jj in range(4 * q, j + 1):
                                    row = NT + jj if jj < NS - 1 else NPT
                                    last = nc.tensor.matmul(ps[:, 6 + hh, 0:64], ET[q % 2][:, jj % 4, :], VR[:, row, 64 * hh:64 * hh + 64],
                                                            start=(jj == 0), stop=(jj == NS - 1))
                        last.then_inc(o_ready, 1)

                @block.scalar
                def _(act):
                    own = InOrder(act, act_own)
                    for u in range(NU + 2):
                        src = bank2(u)[:, 0:P * (units[u][1] + 1)] if u < NU else sample[:, 0:NS * P]
                        dst = E[:, u % 2, 0:P * (units[u][1] + 1)] if u < NU else flat
                        act.wait_ge(max_done, u + 1)
                        if u < NU and u >= 2:
                            act.wait_ge(turned, u - 1)
                        if u == NU:
                            act.wait_ge(turned, NU)
                        nc.scalar.activation(dst, src, ACT.Exp, bias=nm[:, u:u + 1], scale=scale, accum_out=rsum[:, u:u + 1]).then_inc(exps_done, 1)
                        if u < NU:
                            act.wait_ge(turned, u + 1)
                            if u >= 2:
                                act.wait_ge(o_ready, u - 1)
                            n = min(units[u][1] + 1, 4)
                            nc.scalar.activation(ET[u % 2][:, 0:n, :].rearrange("p j n -> p (j n)"), ps[:, 4, 0:P * n], ACT.Copy).then_inc(turned_copied_a, 1)
                        else:
                            for q in range(NGS):
                                act.wait_ge(turned, NU + NGS * (u - NU) + q + 1)
                                if q < 2:
                                    act.wait_ge(o_ready, u)
                                n = min(4, NS - 4 * q)
                                nc.scalar.activation(ET[q % 2][:, 0:n, :].rearrange("p j n -> p (j n)"), ps[:, 5, 0:P * n], ACT.Copy).then_inc(turned_copied_a, 1)

                @block.vector
                def _(dve):
                    own = InOrder(dve, vec)

                    def maximum(u):
                        dve.wait_ge(scores_ready, u + 1)
                        if u < NU:
                            n = P * (units[u][1] + 1)
                            src = bank2(u)[:, 0:n]
                            own(V.memset(src[0:64, n - 64:n], NEG))
                        else:
                            src = sample[:, 0:NS * P]
                        own(V.tensor_reduce(mx[:, u:u + 1], src, AX.X, ALU.max))
                        own(V.tensor_scalar(nm[:, u:u + 1], mx[:, u:u + 1], -scale, None, ALU.mult), max_done)

                    def finish(u):
                        hh, i = units[u] if u < NU else (u - NU, NPT)
                        dve.wait_ge(o_ready, u + 1)
                        own(V.reciprocal(rsum[:, u:u + 1], rsum[:, u:u + 1]))
                        own(V.tensor_scalar(OR[:, i, 64 * hh:64 * hh + 64], ps[:, 6 + u % 2, 0:64], rsum[:, u:u + 1], None, ALU.mult), o_done)

                    maximum(0)
                    for u in range(NU):
                        if u + 1 < NU:
                            maximum(u + 1)
                        dve.wait_ge(turned, u + 1)
                        n = units[u][1] + 1
                        if n > 4:
                            if u >= 2:
                                dve.wait_ge(o_ready, u - 1)
                            V.tensor_copy(ET[u % 2][:, 4:n, :].rearrange("p j n -> p (j n)"), ps[:, 5, 0:P * (n - 4)]).then_inc(turned_copied_v, 1)
                        else:
                            V.engine_nop().then_inc(turned_copied_v, 1)
                        finish(u)
                    for u in (NU, NU + 1):
                        maximum(u)
                        finish(u)

        gate_and_store(nc, S, A, l, h, ps, con, hT, yg, 1, G_ZB, rows=OR)


def stick_breaking(nc, S, A, O, l, ps, con, hT, yg):
    V = nc.vector
    names = ("w_loaded", "projected", "copied", "stored0", "stored1")
    with S.stage(*names) as (block, sb, (w_loaded, projected, copied, stored0, stored1)):
        w = sb("w_sb_values", [P, KD, W0])
        rows = [sb(f"value_rows{i}", [P, W0]) for i in range(2)]
        stored = (stored0, stored1)

        @block.sync
        def _(sp):
            sp.dma_start(w[:, :, :], A["w_sv"][l]).then_inc(w_loaded, 16)
            for i in range(NT):
                sp.wait_ge(copied, i + 1)
                sp.dma_start(O["sbv"][l, P * i:P * i + P, :], rows[i % 2][:, :]).then_inc(stored[i % 2], 16)
            sp.wait_ge(stored0, 16 * ((NT + 1) // 2))
            sp.wait_ge(stored1, 16 * (NT // 2))

        @block.tensor
        def _(pe):
            pe.wait_ge(w_loaded, 16)
            for i in range(NT):
                if i >= 2:
                    pe.wait_ge(copied, i - 1)
                for k in range(KD):
                    last = nc.tensor.matmul(ps[:, i % 2, :], hT[:, k, P * i:P * i + P], w[:, k, :], start=(k == 0), stop=(k == KD - 1))
                last.then_inc(projected, 1)

        @block.scalar
        def _(act):
            for i in range(NT):
                act.wait_ge(projected, i + 1)
                if i >= 2:
                    act.wait_ge(stored[i % 2], 16 * (i // 2))
                nc.scalar.activation(rows[i % 2][:, :], ps[:, i % 2, :], ACT.Copy).then_inc(copied, 1)

    with nc.Fori(0, HP) as h:
        stick_pair(nc, S, A, O, l, h, ps, con, hT, yg)


def stick_pair(nc, S, A, O, l, h, ps, con, hT, yg):
    ident = con("ident")
    V = nc.vector
    with ExitStack() as ctx:
        OT = ctx.enter_context(nc.sbuf_tensor("sb_outT", [P, T], F32))
        with ExitStack() as inner:
            def hold(name, shape):
                return inner.enter_context(nc.sbuf_tensor(name, shape, F32))

            K = hold("sb_keysT", [P, T])
            Q = hold("sb_queriesT", [P, 2, T])
            KC = hold("sb_cached_keysT", [P, NB * PAST])
            VR = hold("sb_values", [P, NPT, P])
            VC = hold("sb_cached_values", [P, NB * PAST // P, P])
            VN = hold("sb_new_values", [TS, NB, P])

            names = ("w0_loaded", "w1_loaded", "held_loaded", "projected", "copied", "stored")
            with S.stage(*names) as (block, sb, (w0_loaded, w1_loaded, held_loaded, projected, copied, stored)):
                w = [sb(f"w_piece{i}", [P, KD, P]) for i in range(2)]

                @block.sync
                def _(sp):
                    sp.dma_start(w[0][:, :, :], A["w_cols"][l, G_SQ + h]).then_inc(w0_loaded, 16)
                    sp.dma_start(w[1][:, :, :], A["w_cols"][l, G_SK + h]).then_inc(w1_loaded, 16)
                    sp.dma_start(KC[:, :], A["sbkT"][l, h]).then_inc(held_loaded, 16)
                    sp.dma_start(VC[:, :, :], A["sbv"][l, h]).then_inc(held_loaded, 16)
                    own = O["sbv"][l].rearrange("t (h n) -> h t n", n=P)[h]
                    sp.dma_start(VR[:, :, :], own[0:TP, :].rearrange("(i p) n -> p i n", p=P)).then_inc(held_loaded, 16)
                    sp.dma_start(VN[:, :, :], own[TP:T, :].rearrange("(b t) n -> t b n", t=TS)).then_inc(held_loaded, 16)
                    sp.wait_ge(copied, 2 * NTG)
                    sp.dma_start(O["sbkT"][l, h], K[:, :]).then_inc(stored, 16)
                    sp.wait_ge(stored, 16)
                    sp.wait_ge(held_loaded, 64)

                @block.tensor
                def _(pe):
                    pe.wait_ge(w0_loaded, 16)
                    project(nc, pe, ps, (0, 1, 2, 3, 4, 5), w[0], hT, projected, copied, 0)
                    pe.wait_ge(w1_loaded, 16)
                    project(nc, pe, ps, (0, 1, 2, 3, 4, 5), w[1], hT, projected, copied, NTG)

                @block.scalar
                def _(act):
                    for g in range(2 * NTG):
                        c = slice(TG * (g % NTG), TG * (g % NTG) + TG)
                        act.wait_ge(projected, g + 1)
                        if g < NTG:
                            nc.scalar.activation(Q[:, 0, c], ps[:, g, 0:TG], ACT.Copy, scale=con("headscale")[:, 0:1])
                            nc.scalar.activation(Q[:, 1, c], ps[:, g, 0:TG], ACT.Copy, scale=con("headscale")[:, 1:2]).then_inc(copied, 1)
                        else:
                            nc.scalar.activation(K[:, c], ps[:, g, 0:TG], ACT.Copy).then_inc(copied, 1)

            names = ("z_ready", "log_done", "sp_done", "total_done", "logit_ready", "weight_done", "o_ready", "o_copied", "vec", "act_own", "pool_own")
            with S.stage(*names) as (block, sb, (z_ready, log_done, sp_done, total_done, logit_ready, weight_done, o_ready, o_copied, vec, act_own, pool_own)):
                E = [sb(f"exp_abs{i}", [P, 512]) for i in range(3)]
                SP = [sb(f"softplus{i}", [P, 512]) for i in range(3)]
                W = [sb(f"weights{i}", [P, 512]) for i in range(3)]
                R = [[sb(f"later_sum{hh}{i}", [P, 512]) for i in range(2)] for hh in range(2)]
                units = [(g, kt, hh) for g in range(2) for kt in reversed(range(4 * g + 4)) for hh in range(2)]
                NU = len(units)

                def span(u):
                    g, kt, hh = units[u]
                    return max(0, P * (kt - 4 * g)), kt >= 4 * g

                def turn(u):
                    g, kt, hh = units[u]
                    return 4 * g + 3 - kt

                @block.tensor
                def _(pe):
                    def z(u):
                        g, kt, hh = units[u]
                        c, _ = span(u)
                        if u >= 6:
                            pe.wait_ge(weight_done, u - 5)
                        nc.tensor.matmul(ps[:, u % 6, c:512], K[:, P * kt:P * kt + P], Q[:, hh, 512 * g + c:512 * g + 512],
                                         start=True, stop=False, skip_group_check=True).then_inc(z_ready, 1)

                    def logits(u):
                        g, kt, hh = units[u]
                        c, diagonal = span(u)
                        pe.wait_ge(sp_done, u + 1)
                        if turn(u):
                            pe.wait_ge(total_done, u - 1)
                            nc.tensor.matmul(ps[:, u % 6, c:512], con("negones"), R[hh][turn(u) % 2][:, c:512], start=False, stop=False, skip_group_check=True)
                        if diagonal:
                            nc.tensor.matmul(ps[:, u % 6, c:c + P], ident, con("sbneg"), start=False, stop=False, skip_group_check=True)
                        nc.tensor.matmul(ps[:, u % 6, c:512], con("negtri"), SP[u % 3][:, c:512], start=False, stop=True, skip_group_check=True).then_inc(logit_ready, 1)

                    def values(u):
                        g, kt, hh = units[u]
                        c, _ = span(u)
                        pe.wait_ge(weight_done, u + 1)
                        if g == 1 and kt == 7:
                            pe.wait_ge(o_copied, hh + 1)
                        ins = nc.tensor.matmul(ps[64 * hh:64 * hh + 64, 6 + hh, c:512], VR[:, kt, 64 * hh:64 * hh + 64], W[u % 3][:, c:512],
                                               start=(kt == 4 * g + 3), stop=(kt == 0), skip_group_check=True)
                        ins.then_inc(o_ready, 1)

                    for u in range(2):
                        z(u)
                    for u in range(NU):
                        if u + 2 < NU:
                            z(u + 2)
                        logits(u)
                        if u >= 1:
                            values(u - 1)
                    values(NU - 1)

                @block.scalar
                def _(act):
                    own = InOrder(act, act_own)
                    nc.scalar.preload_act_table_set("natural_log_exp_and_others")

                    def logs(u):
                        c, _ = span(u)
                        act.wait_ge(z_ready, u + 1)
                        if u >= 3:
                            act.wait_ge(sp_done, u - 2)
                        own(nc.scalar.activation(E[u % 3][:, c:512], ps[:, u % 6, c:512], ACT.Abs))
                        own(nc.scalar.activation(E[u % 3][:, c:512], E[u % 3][:, c:512], ACT.Exp, scale=-1.0))
                        nc.scalar.activation(E[u % 3][:, c:512], E[u % 3][:, c:512], ACT.Ln, bias=1.0).then_inc(log_done, 1)

                    logs(0)
                    for u in range(NU):
                        g, kt, hh = units[u]
                        if u + 1 < NU:
                            logs(u + 1)
                        c, _ = span(u)
                        act.wait_ge(logit_ready, u + 1)
                        if u >= 3:
                            act.wait_ge(o_ready, u - 2)
                        nc.scalar.activation(W[u % 3][:, c:512], ps[:, u % 6, c:512], ACT.Exp).then_inc(weight_done, 1)
                        if kt == 0:
                            act.wait_ge(o_ready, u + 1)
                            hc = slice(64 * hh, 64 * hh + 64)
                            nc.scalar.activation(OT[hc, 512 * g:512 * g + 512], ps[hc, 6 + hh, :], ACT.Copy).then_inc(o_copied, 1)

                @block.vector
                def _(dve):
                    own = InOrder(dve, vec)

                    for u in range(NU):
                        g, kt, hh = units[u]
                        c, diagonal = span(u)
                        dve.wait_ge(log_done, u + 1)
                        if u >= 3:
                            dve.wait_ge(logit_ready, u - 2)
                            dve.wait_ge(total_done, u - 2)
                        if diagonal:
                            own(V.scalar_tensor_tensor(SP[u % 3][:, c:512], ps[:, u % 6, c:512], 0.0, E[u % 3][:, c:512], ALU.max, ALU.add))
                            own(V.tensor_tensor(SP[u % 3][:, c:c + P], SP[u % 3][:, c:c + P], con("sbkeep"), ALU.mult), sp_done)
                        else:
                            own(V.scalar_tensor_tensor(SP[u % 3][:, c:512], ps[:, u % 6, c:512], 0.0, E[u % 3][:, c:512], ALU.max, ALU.add), sp_done)

                @block.gpsimd
                def _(pool):
                    own = InOrder(pool, pool_own)
                    for u in range(NU):
                        g, kt, hh = units[u]
                        c, _ = span(u)
                        r0, r1 = R[hh][turn(u) % 2], R[hh][(turn(u) + 1) % 2]
                        if u < 2:
                            for r in R[hh]:
                                own(nc.gpsimd.memset(r[:, :], 0.0))
                        if kt == 4 * g + 3 and g:
                            pool.wait_ge(logit_ready, u)
                            for r in R[hh]:
                                own(nc.gpsimd.memset(r[:, :], 0.0))
                        pool.wait_ge(sp_done, u + 1)
                        if u >= 2:
                            pool.wait_ge(logit_ready, u - 1)
                        nc.gpsimd.tensor_tensor(r1[:, c:512], r0[:, c:512], SP[u % 3][:, c:512], ALU.add).then_inc(total_done, 1)
                        pool.wait_ge(total_done, u + 1)

            names = ("z_ready", "log_done", "sp_done", "logit_ready", "weight_done", "o_ready", "o_copied", "masks_loaded", "vec", "act_own")
            with S.stage(*names) as (block, sb, (z_ready, log_done, sp_done, logit_ready, weight_done, o_ready, o_copied, masks_loaded, vec, act_own)):
                E = [sb(f"exp_abs{hh}", [P, 3, P]) for hh in range(2)]
                SPS = [sb(f"softplus{hh}", [P, 3, P]) for hh in range(2)]
                W = [sb(f"weights{hh}", [P, 3, P]) for hh in range(2)]
                cross = sb("cross", [TS, 2, P])

                def part(t, j):
                    return t[0:TS, j, :] if j == 0 else t[:, j, :]

                def bank(hh, j):
                    return ps[0:TS, 3 * hh, 0:P] if j == 0 else ps[:, 3 * hh + j, 0:P]

                @block.sync
                def _(sp):
                    sp.dma_start(cross[:, 0, :], con("cross")[0:TS, :]).then_inc(masks_loaded, 16)
                    sp.dma_start(cross[:, 1, :], con("crossneg")[0:TS, :]).then_inc(masks_loaded, 16)

                @block.tensor
                def _(pe):
                    mm = nc.tensor.matmul
                    for hh in range(2):
                        for j in range(3):
                            for b in range(NB):
                                tok = slice(TP + TS * b, TP + TS * b + TS)
                                a = PAST * b + P * (2 - j)
                                keys = K[:, tok] if j == 0 else KC[:, a:a + P]
                                last = mm(bank(hh, j)[:, TS * b:TS * b + TS], keys, Q[:, hh, tok], start=(b == 0), stop=False, skip_group_check=True)
                        last.then_inc(z_ready, 1)
                    pe.wait_ge(masks_loaded, 32)
                    for hh in range(2):
                        pe.wait_ge(sp_done, hh + 1)
                        sps = SPS[hh]
                        mm(bank(hh, 0), ident[0:TS, 0:TS], cross[:, 1, :], start=False, stop=False, skip_group_check=True)
                        mm(bank(hh, 0), con("negtri")[0:TS, 0:TS], sps[0:TS, 0, :], start=False, stop=True, skip_group_check=True)
                        mm(bank(hh, 1), con("negones")[0:TS, :], sps[0:TS, 0, :], start=False, stop=False, skip_group_check=True)
                        mm(bank(hh, 1), con("negtri"), sps[:, 1, :], start=False, stop=True, skip_group_check=True)
                        mm(bank(hh, 2), con("negones")[0:TS, :], sps[0:TS, 0, :], start=False, stop=False, skip_group_check=True)
                        mm(bank(hh, 2), con("negones"), sps[:, 1, :], start=False, stop=False, skip_group_check=True)
                        mm(bank(hh, 2), con("negtri"), sps[:, 2, :], start=False, stop=True, skip_group_check=True).then_inc(logit_ready, 1)
                    for hh in range(2):
                        hc = slice(64 * hh, 64 * hh + 64)
                        pe.wait_ge(weight_done, hh + 1)
                        for b in range(NB):
                            out = ps[hc, 6 + hh, TS * b:TS * b + TS]
                            q = slice(TS * b, TS * b + TS)
                            mm(out, VN[:, b, hc], W[hh][0:TS, 0, q], start=(b == 0), stop=False, skip_group_check=True)
                            mm(out, VC[:, 2 * b + 1, hc], W[hh][:, 1, q], start=False, stop=False, skip_group_check=True)
                            last = mm(out, VC[:, 2 * b, hc], W[hh][:, 2, q], start=False, stop=True, skip_group_check=True)
                        last.then_inc(o_ready, 1)

                @block.scalar
                def _(act):
                    own = InOrder(act, act_own)
                    nc.scalar.preload_act_table_set("natural_log_exp_and_others")
                    for hh in range(2):
                        act.wait_ge(z_ready, hh + 1)
                        for j in range(3):
                            own(nc.scalar.activation(part(E[hh], j), bank(hh, j), ACT.Abs))
                            own(nc.scalar.activation(part(E[hh], j), part(E[hh], j), ACT.Exp, scale=-1.0))
                            own(nc.scalar.activation(part(E[hh], j), part(E[hh], j), ACT.Ln, bias=1.0), log_done)
                    for hh in range(2):
                        act.wait_ge(logit_ready, hh + 1)
                        for j in range(3):
                            ins = nc.scalar.activation(part(W[hh], j), bank(hh, j), ACT.Exp)
                        ins.then_inc(weight_done, 1)
                    for hh in range(2):
                        hc = slice(64 * hh, 64 * hh + 64)
                        act.wait_ge(o_ready, hh + 1)
                        nc.scalar.activation(OT[hc, TP:T], ps[hc, 6 + hh, 0:P], ACT.Copy).then_inc(o_copied, 1)

                @block.vector
                def _(dve):
                    own = InOrder(dve, vec)
                    dve.wait_ge(masks_loaded, 32)
                    for hh in range(2):
                        dve.wait_ge(log_done, 3 * (hh + 1))
                        for j in range(3):
                            own(V.scalar_tensor_tensor(part(SPS[hh], j), bank(hh, j), 0.0, part(E[hh], j), ALU.max, ALU.add))
                        own(V.tensor_tensor(SPS[hh][0:TS, 0, :], SPS[hh][0:TS, 0, :], cross[:, 0, :], ALU.mult), sp_done)

        gate_and_store(nc, S, A, l, h, ps, con, hT, yg, 2, G_ZC, cols=OT)


def merge(nc, S, A, l, ps, con, hT, yg, gates, X):
    V = nc.vector
    with ExitStack() as ctx:
        M = ctx.enter_context(nc.sbuf_tensor("mergedT", [P, KD, T], F32))
        names = ("y_loaded", "w0_loaded", "w1_loaded", "products", "gate_read", "product_read", "piece_done")
        with S.stage(*names) as (block, sb, (y_loaded, w0_loaded, w1_loaded, products, gate_read, product_read, piece_done)):
            HT = T // 1
            Y = [sb(f"y_branch{b}", [P, HP, HT]) for b in range(2)]
            wg = [sb(f"w_gate{i}", [P, KD, P]) for i in range(2)]
            wb = [sb(f"w_branch{i}", [P, HP, P]) for i in range(2)]
            th = [sb(f"gate_tanh{i}", [P, TG]) for i in range(2)]
            w_loaded = [w0_loaded, w1_loaded]
            units = [(b, n, g) for b in range(3) for n in range(KD) for g in range(NTG)]

            @block.sync
            def _(sp):
                for j in range(3 * KD):
                    b, n = divmod(j, KD)
                    if n == 0:
                        if b == 2:
                            sp.wait_ge(products, NTG * KD)
                        sp.dma_start(Y[b % 2][:, :, :], yg[b].rearrange("h p t -> p h t")).then_inc(y_loaded, 16)
                    if j >= 2:
                        sp.wait_ge(products, NTG * (j - 1))
                    sp.dma_start(wg[j % 2][:, :, :], A["w_cols"][l, G_GATE + KD * b + n]).then_inc(w_loaded[j % 2], 16)
                    sp.dma_start(wb[j % 2][:, :, :], A["w_br"][l, n, :, b]).then_inc(w_loaded[j % 2], 16)

            @block.tensor
            def _(pe):
                for u, (b, n, g) in enumerate(units):
                    j, c = KD * b + n, slice(TG * g, TG * g + TG)
                    if g == 0:
                        pe.wait_ge(w_loaded[j % 2], 32 * (j // 2 + 1))
                        if n == 0:
                            pe.wait_ge(y_loaded, 16 * (b + 1))
                    if u >= 4:
                        pe.wait_ge(product_read, u - 3)
                    for k in range(KD):
                        nc.tensor.matmul(ps[:, 2 * (u % 4), 0:TG], wg[j % 2][:, k, :], hT[:, k, c], start=(k == 0), stop=(k == KD - 1))
                    for k in range(HP):
                        last = nc.tensor.matmul(ps[:, 2 * (u % 4) + 1, 0:TG], wb[j % 2][:, k, :], Y[b % 2][:, k, c], start=(k == 0), stop=(k == HP - 1))
                    last.then_inc(products, 1)

            @block.scalar
            def _(act):
                for u, (b, n, g) in enumerate(units):
                    act.wait_ge(products, u + 1)
                    if u >= 2:
                        act.wait_ge(product_read, u - 1)
                    nc.scalar.activation(th[u % 2][:, :], ps[:, 2 * (u % 4), 0:TG], ACT.Tanh, scale=0.5).then_inc(gate_read, 1)

            @block.vector
            def _(dve):
                own = InOrder(dve, piece_done)
                for u, (b, n, g) in enumerate(units):
                    c = slice(TG * g, TG * g + TG)
                    dve.wait_ge(gate_read, u + 1)
                    if b == 0:
                        own(V.scalar_tensor_tensor(M[:, n, c], th[u % 2][:, :], 1.0, ps[:, 2 * (u % 4) + 1, 0:TG], ALU.add, ALU.mult), product_read)
                    else:
                        own(V.scalar_tensor_tensor(th[u % 2][:, :], th[u % 2][:, :], 1.0, ps[:, 2 * (u % 4) + 1, 0:TG], ALU.add, ALU.mult))
                        own(V.tensor_tensor(M[:, n, c], M[:, n, c], th[u % 2][:, :], ALU.add), product_read)

        names = ("w_loaded", "halved", "products", "read", "added")
        with S.stage(*names) as (block, sb, (w_loaded, halved, products, read, added)):
            w = sb("w_out", [P, KD, D])
            t = [sb(f"update{i}", [P, 512]) for i in range(2)]

            @block.sync
            def _(sp):
                sp.dma_start(w[:, :, :], A["w_out"][l]).then_inc(w_loaded, 16)

            @block.tensor
            def _(pe):
                pe.wait_ge(w_loaded, 16)
                pe.wait_ge(halved, 1)
                for i in range(NT):
                    for n in range(2):
                        u = 2 * i + n
                        if u >= 4:
                            pe.wait_ge(read, u - 3)
                        for k in range(KD):
                            last = nc.tensor.matmul(ps[:, u % 4, :], M[:, k, P * i:P * i + P], w[:, k, 512 * n:512 * n + 512], start=(k == 0), stop=(k == KD - 1))
                        last.then_inc(products, 1)

            @block.vector
            def _(dve):
                own = InOrder(dve, added)
                own(V.tensor_scalar(gates[:, :, :], gates[:, :, :], 0.5, None, ALU.mult), halved)
                for u in range(2 * NT):
                    i, c = u // 2, slice(512 * (u % 2), 512 * (u % 2) + 512)
                    dve.wait_ge(products, u + 1)
                    own(V.tensor_tensor(t[u % 2][:, :], ps[:, u % 4, :], gates[:, int(i == NPT), c], ALU.mult), read)
                    own(V.tensor_tensor(X[:, i, c], X[:, i, c], t[u % 2][:, :], ALU.add))


def pieces(w):
    k, n = w.shape[-2:]
    return w.reshape(*w.shape[:-2], k // P, P, n // P, P).transpose(0, 3, 2, 1, 4)


def rows_first(w):
    return w.reshape(L, w.shape[1] // P, P, w.shape[2]).transpose(0, 2, 1, 3)


def lay_out(i):
    cat = np.concatenate
    col = {}
    at = 0
    for n, wd in (("shift", RW), ("zA", W0), ("lat", QL + KVL + RP), ("zB", W0), ("sq", W0), ("sk", W0), ("sv", W0), ("zC", W0), ("gates", 3 * D)):
        col[n] = i["w_in"][:, :, at:at + wd]
        at += wd
    a = {}
    a["x_prompt"], a["x_sample"] = i["x_prompt"], i["x_sample"]
    a["c_all"] = cat([i["c_prompt"], i["c_sample"]], 0)
    a["w_ada"] = i["w_ada"].reshape(L, KD, P, 6, 512).transpose(0, 3, 2, 1, 4)
    a["b_ada"] = i["b_ada"][:, None, :]
    a["norm_g"] = i["norm_g"].reshape(L, KD, P).transpose(0, 2, 1)
    a["w_cols"] = pieces(cat([col[n] for n in ("shift", "zA", "zB", "sq", "sk", "zC", "gates")], 2))
    a["w_lat"] = rows_first(col["lat"])
    a["w_sv"] = rows_first(col["sv"])
    a["mu_lora"] = i["rwkv_mu"][:, 3 * W0:, None]
    a["shift0"] = i["state_rwkv_shift"].reshape(L, NB, 13, P).transpose(0, 2, 3, 1)
    vec = [i["rwkv_mu"][:, W0 * j:W0 * j + W0] for j in range(3)]
    vec += [i["rwkv_" + n] for n in ("w0", "a0", "k_k", "k_a", "r_k", "gn_g", "gn_b")]
    a["rw_par"] = np.stack(vec, -1).reshape(L, HP, P, 10)
    a["w_lora"] = cat([i["rwkv_w_up"], i["rwkv_a_up"]], 1).reshape(L, P, HP, P).transpose(0, 2, 1, 3)
    a["state0"] = i["state_rwkv_wkv"].reshape(L, NB, HP, 2, 64, 64).transpose(0, 2, 3, 5, 1, 4).reshape(L, HP, P, NB * 64)
    uq = i["mla_w_uq"].reshape(L, QL, HP, 2, QK)
    a["w_uq"] = cat([uq[..., :64].reshape(L, QL, HP, P), uq[..., 64:].reshape(L, QL, HP, 64)], -1).reshape(L, 3, P, HP, 192).transpose(0, 3, 2, 1, 4)
    ukv = i["mla_w_ukv"].reshape(L, KVL, HP, 2, 2, 64).transpose(0, 1, 2, 4, 3, 5).reshape(L, 2, P, HP, 2 * P)
    a["w_ukv"] = ukv.transpose(0, 3, 2, 1, 4)
    a["lat_rows"] = cat([i["mla_q_norm"], i["mla_kv_norm"], i["mla_kn_rope"]], 1)[:, None, :]
    two = lambda x, n: np.tile(x, (1, n))
    z = np.zeros((L, P), np.float32)
    z[:, :64] = two(i["mla_qn_rope"], 2)
    zk = np.zeros((L, P), np.float32)
    zk[:, :RP] = i["mla_kn_rope"]
    a["lat_par"] = np.stack([two(i["mla_qn_nope"], 2), z, two(i["mla_kn_nope"], 2), zk], -1)
    a["ckvT"] = i["cache_mla_ckv"].reshape(L, NB * PAST, 2, P).transpose(0, 3, 2, 1)
    a["krT"] = i["cache_mla_krope"].reshape(L, NB * PAST, RP).transpose(0, 2, 1)
    a["sbkT"] = i["cache_sb_k"].reshape(L, NB * PAST, HP, P).transpose(0, 2, 3, 1)
    a["sbv"] = i["cache_sb_v"].reshape(L, NB * PAST // P, P, HP, P).transpose(0, 3, 2, 1, 4)
    br = np.stack([i["w_br_rwkv"], i["w_br_mla"], i["w_br_sb"]], 1)
    a["w_br"] = br.reshape(L, 3, HP, P, KD, P).transpose(0, 4, 3, 1, 2, 5)
    a["w_out"] = rows_first(i["w_out"])
    a["consts"] = shape_constants()
    return {n: np.ascontiguousarray(v) for n, v in a.items()}


OUT_SHAPES = {
    "y_prompt": (1, TP, D), "y_sample": (NB, TS, D),
    "wkv_p": (L, HP, P, 64), "wkv_s": (L, HP, P, NB * 64), "shift_p": (L, 13, P, 1), "shift_s": (L, 13, P, NB),
    "ckv": (L, T, KVL), "kropeT": (L, RP, T), "sbkT": (L, HP, P, T), "sbv": (L, T, W0),
}


def as_reference(r):
    wkv_p = r["wkv_p"].reshape(L, HP, 2, 64, 1, 64).transpose(0, 4, 1, 2, 5, 3).reshape(L, 1, 8, 64, 64)
    wkv_s = r["wkv_s"].reshape(L, HP, 2, 64, NB, 64).transpose(0, 4, 1, 2, 5, 3).reshape(L, NB, 8, 64, 64)
    shift_p = r["shift_p"].reshape(L, 1, 1, RW)
    shift_s = r["shift_s"].reshape(L, RW, NB).transpose(0, 2, 1).reshape(L, NB, 1, RW)
    krope = r["kropeT"].transpose(0, 2, 1)
    sbk = r["sbkT"].reshape(L, W0, T).transpose(0, 2, 1).reshape(L, T, 8, 64)
    sbv = r["sbv"].reshape(L, T, 8, 64)
    p = lambda v: v[:, :TP].reshape(L, 1, TP, *v.shape[2:])
    s = lambda v: v[:, TP:].reshape(L, NB, TS, *v.shape[2:])
    out = (r["y_prompt"], r["y_sample"], wkv_p, shift_p, p(r["ckv"]), p(krope), p(sbk), p(sbv),
           wkv_s, shift_s, s(r["ckv"]), s(krope), s(sbk), s(sbv))
    return tuple(np.ascontiguousarray(v) for v in out)


def kernel(**inputs):
    import concourse.bacc as bacc
    from concourse.bass_utils import run_bass_kernel_spmd

    arrays = lay_out({n: np.asarray(v) for n, v in inputs.items()})
    nc = bacc.Bacc("TRN2", target_bir_lowering=False, num_devices=1)
    A = {n: nc.dram_tensor("in_" + n, v.shape, F32, kind="ExternalInput").ap() for n, v in arrays.items()}
    O = {n: nc.dram_tensor("out_" + n, s, F32, kind="ExternalOutput").ap() for n, s in OUT_SHAPES.items()}
    build(nc, A, O)
    r = run_bass_kernel_spmd(nc, [{"in_" + n: v for n, v in arrays.items()}], core_ids=[0]).results[0]
    return as_reference({n: r["out_" + n] for n in OUT_SHAPES})
```
